# Optimizing a Trainium2 kernel written in Bass

```python
import jax, jax.numpy as jnp
from jax import lax
import numpy as np

D_MODEL = 1024
BATCH = 1
SEQ = 1024
DEPTH = 2
DEC_BATCH = 8
DEC_SEQ = 8
PAST_LEN = 1024
PAGE_SIZE = 128

N_MIXERS = 2
N_A = (DEPTH + 1) // 2
N_B = DEPTH // 2
RW_HEAD = 64
RW_HEADS = D_MODEL // RW_HEAD
RW_DECAY_LORA = 64
RW_AAA_LORA = 64
RW_GATE_LORA = 160
RW_GN_EPS = 64e-5
ATT_GROUPS = ((128, 1), (512, 4), (2048, 16))
N_GROUPS = 3
ATT_HEADS = 8
ATT_HEAD_DIM = 64
ATT_WIDTH = ATT_HEADS * ATT_HEAD_DIM
ATT_SCALE = ATT_HEAD_DIM ** -0.5
ROT_DIM = ATT_HEAD_DIM // 4
ROPE_THETA = 500000.0
D_FF = 2816
CONV_W = 3
NORM_EPS = 1e-6
F32 = jnp.float32

kernel_name = 'hybrid_rwkv7_dilated_swa_convffn_step'

def rmsnorm(x, g):
    xf = x.astype(F32)
    y = xf * lax.rsqrt(jnp.mean(xf * xf, axis=-1, keepdims=True) + NORM_EPS)
    return (y * g.astype(F32)).astype(x.dtype)

def rope(x, pos):
    half = ROT_DIM // 2
    inv = jnp.power(ROPE_THETA, -jnp.arange(half, dtype=F32) / half)
    ang = pos.astype(F32)[:, None] * inv[None, :]
    cos = jnp.cos(ang)[None, :, None, :]
    sin = jnp.sin(ang)[None, :, None, :]
    xf = x.astype(F32)
    x1, x2 = xf[..., :half], xf[..., half:ROT_DIM]
    out = jnp.concatenate([x1 * cos - x2 * sin, x2 * cos + x1 * sin, xf[..., ROT_DIM:]], axis=-1)
    return out.astype(x.dtype)

def rwkv7_mix(xn, shift_prev, s0, p):
    (mu, wr, wk, wv, wo, w0, w1, w2, a0, a1, a2, g1, g2, k_k, k_a, r_k, lnx_g, lnx_b) = p
    b, t, d = xn.shape
    h, n = RW_HEADS, RW_HEAD
    prev = jnp.concatenate([shift_prev[:, None, :].astype(xn.dtype), xn[:, :-1]], axis=1)
    xx = prev - xn
    xr, xw, xk, xv, xa, xg = [xn + xx * mu[i] for i in range(6)]
    r = xr @ wr
    k = xk @ wk
    v = xv @ wv
    w = -jax.nn.softplus(-(w0 + jnp.tanh(xw @ w1) @ w2)) - 0.5
    a = jax.nn.sigmoid(a0 + (xa @ a1) @ a2)
    g = jax.nn.sigmoid(xg @ g1) @ g2
    heads = lambda z: z.reshape(b, t, h, n).astype(F32)
    kk = heads(k * k_k)
    kk = kk / jnp.maximum(jnp.linalg.norm(kk, axis=-1, keepdims=True), 1e-12)
    k = k * (1 + (a - 1) * k_a)
    r_h, k_h, v_h, a_h = heads(r), heads(k), heads(v), heads(a)
    decay = jnp.exp(-jnp.exp(heads(w)))

    def step(S, inp):
        r_t, d_t, k_t, v_t, kk_t, a_t = inp
        sk = jnp.einsum('bhvk,bhk->bhv', S, kk_t)
        S = (S * d_t[:, :, None, :] - sk[..., None] * (kk_t * a_t)[:, :, None, :]
             + v_t[..., None] * k_t[:, :, None, :])
        return S, jnp.einsum('bhvk,bhk->bhv', S, r_t)

    tm = lambda z: jnp.swapaxes(z, 0, 1)
    s_fin, ys = lax.scan(step, s0.astype(F32),
                         (tm(r_h), tm(decay), tm(k_h), tm(v_h), tm(kk), tm(a_h)))
    y = tm(ys)
    mean = jnp.mean(y, axis=-1, keepdims=True)
    var = jnp.mean(jnp.square(y - mean), axis=-1, keepdims=True)
    y = ((y - mean) * lax.rsqrt(var + RW_GN_EPS)).reshape(b, t, d) * lnx_g + lnx_b
    bonus = jnp.sum(r_h * k_h * r_k, axis=-1, keepdims=True) * v_h
    y = (y + bonus.reshape(b, t, d)).astype(xn.dtype)
    out = (y * g) @ wo
    return out, xn[:, -1], s_fin.astype(s0.dtype)

def dilated_group_prompt(q, k, v, window, dil):
    b, s, h, e = q.shape
    blk = window // dil
    n_sub = s // dil
    nb = -(-n_sub // blk)
    lp = nb * blk

    def sub(z):
        z = z.reshape(b, n_sub, dil, h, e).transpose(0, 2, 1, 3, 4)
        return jnp.pad(z, ((0, 0), (0, 0), (0, lp - n_sub), (0, 0), (0, 0)))

    def band(z):
        z = jnp.pad(sub(z), ((0, 0), (0, 0), (blk, 0), (0, 0), (0, 0))).reshape(b, dil, nb + 1, blk, h, e)
        return jnp.concatenate([z[:, :, :-1], z[:, :, 1:]], axis=3)

    qb = sub(q).reshape(b, dil, nb, blk, h, e)
    kb, vb = band(k), band(v)
    sc = jnp.einsum('bdnqhe,bdnkhe->bdnqhk', qb, kb, preferred_element_type=F32) * ATT_SCALE
    qi = jnp.arange(blk)[:, None]
    kj = jnp.arange(2 * blk)[None, :]
    dist = qi + blk - kj
    kidx = jnp.arange(nb)[:, None, None] * blk + kj[None] - blk
    valid = (dist >= 0)[None] & (dist <= blk)[None] & (kidx >= 0)
    sc = jnp.where(valid[None, None, :, :, None, :], sc, -jnp.inf)
    lse = jax.nn.logsumexp(sc, axis=-1)
    pr = jnp.exp(sc - lse[..., None])
    o = jnp.einsum('bdnqhk,bdnkhe->bdnqhe', pr, vb.astype(F32))
    o = o.reshape(b, dil, lp, h, e)[:, :, :n_sub].transpose(0, 2, 1, 3, 4).reshape(b, s, h, e)
    lse = lse.reshape(b, dil, lp, h)[:, :, :n_sub].transpose(0, 2, 1, 3).reshape(b, s, h)
    return o, lse

def dilated_group_sample(q, k_all, v_all, window, dil, offset):
    t = q.shape[1]
    nk = window // dil + 1
    idx = offset + jnp.arange(t)[:, None] - dil * jnp.arange(nk)[None, :]
    valid = idx >= 0
    idx = jnp.maximum(idx, 0)
    kg = jnp.take(k_all, idx, axis=1)
    vg = jnp.take(v_all, idx, axis=1)
    sc = jnp.einsum('bthe,btjhe->bthj', q, kg, preferred_element_type=F32) * ATT_SCALE
    sc = jnp.where(valid[None, :, None, :], sc, -jnp.inf)
    lse = jax.nn.logsumexp(sc, axis=-1)
    pr = jnp.exp(sc - lse[..., None])
    o = jnp.einsum('bthj,btjhe->bthe', pr, vg.astype(F32))
    return o, lse

def dilated_attention(xn, pos, bufs, wqkv, wo):
    b, t, _ = xn.shape
    qkv = (xn @ wqkv).reshape(b, t, 3, N_GROUPS, ATT_HEADS, ATT_HEAD_DIM)
    outs, lses, new = [], [], []
    for gi in range(N_GROUPS):
        window, dil = ATT_GROUPS[gi]
        q = rope(qkv[:, :, 0, gi], pos)
        k = rope(qkv[:, :, 1, gi], pos)
        v = qkv[:, :, 2, gi]
        if bufs is None:
            o, lse = dilated_group_prompt(q, k, v, window, dil)
            keep = min(window, t)
            new.append(jnp.stack([k[:, t - keep:], v[:, t - keep:]], axis=2))
        else:
            buf = bufs[gi].astype(k.dtype)
            k_all = jnp.concatenate([buf[:, :, 0], k], axis=1)
            v_all = jnp.concatenate([buf[:, :, 1], v], axis=1)
            o, lse = dilated_group_sample(q, k_all, v_all, window, dil, buf.shape[1])
            new.append(jnp.stack([k, v], axis=2))
        outs.append(o)
        lses.append(lse)
    wts = jax.nn.softmax(jnp.stack(lses), axis=0)
    o = jnp.sum(wts[..., None] * jnp.stack(outs), axis=0)
    y = o.reshape(b, t, ATT_WIDTH).astype(xn.dtype) @ wo
    return y, new

def conv_ffn(xn, prev, wup, cw, cb, wdown):
    t = xn.shape[1]
    hid = xn @ wup
    hp = jnp.concatenate([prev.astype(hid.dtype), hid], axis=1)
    c = cb
    for j in range(CONV_W):
        c = c + hp[:, j:j + t] * cw[j]
    gate, val = jnp.split(c, 2, axis=-1)
    out = (jax.nn.gelu(gate, approximate=True) * val) @ wdown
    return out, hp[:, t:]

def run_trunk(x, pos, shift0, wkv0, kv_bufs, conv0, norm_g, rw, at_wqkv, at_wo, ff):
    new_shift, new_wkv, new_conv = [], [], []
    new_kv = [[], [], []]
    ia = 0
    ib = 0
    for layer in range(DEPTH):
        g = norm_g[layer]
        hn = rmsnorm(x, g[0])
        if layer % N_MIXERS == 0:
            mo, sh, st = rwkv7_mix(hn, shift0[ia], wkv0[ia], [p[ia] for p in rw])
            new_shift.append(sh)
            new_wkv.append(st)
            ia += 1
        else:
            bufs = None if kv_bufs is None else [buf[ib] for buf in kv_bufs]
            mo, kvs = dilated_attention(hn, pos, bufs, at_wqkv[ib], at_wo[ib])
            for gi in range(N_GROUPS):
                new_kv[gi].append(kvs[gi])
            ib += 1
        x = x + rmsnorm(mo, g[1])
        hn = rmsnorm(x, g[2])
        fo, cs = conv_ffn(hn, conv0[layer], ff[0][layer], ff[1][layer], ff[2][layer], ff[3][layer])
        new_conv.append(cs)
        x = x + rmsnorm(fo, g[3])
    kv_out = [jnp.stack(kv) for kv in new_kv]
    return x, jnp.stack(new_shift), jnp.stack(new_wkv), kv_out, jnp.stack(new_conv)

def setup_inputs(seed: int = 0) -> dict:
    key = jax.random.key(seed)
    ks = iter(jax.random.split(key, 64))
    nrm = lambda shape, scale=1.0: jax.random.normal(next(ks), shape, F32) * scale
    D = D_MODEL
    H, N = RW_HEADS, RW_HEAD
    F2 = 2 * D_FF
    wl = [min(w, PAST_LEN) for (w, _) in ATT_GROUPS]
    kvshape = lambda L: (N_B, DEC_BATCH, L, 2, ATT_HEADS, ATT_HEAD_DIM)
    return {
        'x_prompt': nrm((BATCH, SEQ, D)),
        'x_sample': nrm((DEC_BATCH, DEC_SEQ, D)),
        'state_shift': nrm((N_A, DEC_BATCH, D)),
        'state_wkv': nrm((N_A, DEC_BATCH, H, N, N), 0.3),
        'cache_kv_w128': nrm(kvshape(wl[0])),
        'cache_kv_w512': nrm(kvshape(wl[1])),
        'cache_kv_w2048': nrm(kvshape(wl[2])),
        'state_conv': nrm((DEPTH, DEC_BATCH, CONV_W - 1, F2)),
        'norm_g': 1.0 + nrm((DEPTH, 4, D), 0.05),
        'rw_mu': jax.random.uniform(next(ks), (N_A, 6, D), F32),
        'rw_wr': nrm((N_A, D, D), D ** -0.5),
        'rw_wk': nrm((N_A, D, D), D ** -0.5),
        'rw_wv': nrm((N_A, D, D), D ** -0.5),
        'rw_wo': nrm((N_A, D, D), D ** -0.5),
        'rw_w0': nrm((N_A, D), 0.5),
        'rw_w1': nrm((N_A, D, RW_DECAY_LORA), D ** -0.5),
        'rw_w2': nrm((N_A, RW_DECAY_LORA, D), 0.3 * RW_DECAY_LORA ** -0.5),
        'rw_a0': nrm((N_A, D), 0.5),
        'rw_a1': nrm((N_A, D, RW_AAA_LORA), D ** -0.5),
        'rw_a2': nrm((N_A, RW_AAA_LORA, D), 0.3 * RW_AAA_LORA ** -0.5),
        'rw_g1': nrm((N_A, D, RW_GATE_LORA), D ** -0.5),
        'rw_g2': nrm((N_A, RW_GATE_LORA, D), RW_GATE_LORA ** -0.5),
        'rw_kk': 0.85 + nrm((N_A, D), 0.05),
        'rw_ka': 1.0 + nrm((N_A, D), 0.05),
        'rw_rk': nrm((N_A, H, N), 0.1),
        'rw_lnx_g': 1.0 + nrm((N_A, D), 0.05),
        'rw_lnx_b': nrm((N_A, D), 0.02),
        'at_wqkv': nrm((N_B, D, 3 * N_GROUPS * ATT_WIDTH), D ** -0.5),
        'at_wo': nrm((N_B, ATT_WIDTH, D), ATT_WIDTH ** -0.5),
        'ff_wup': nrm((DEPTH, D, F2), D ** -0.5),
        'ff_conv_w': nrm((DEPTH, CONV_W, F2), CONV_W ** -0.5),
        'ff_conv_b': nrm((DEPTH, F2), 0.02),
        'ff_wdown': nrm((DEPTH, D_FF, D), D_FF ** -0.5),
    }

def reference(x_prompt, x_sample, state_shift, state_wkv, cache_kv_w128, cache_kv_w512,
              cache_kv_w2048, state_conv, norm_g, rw_mu, rw_wr, rw_wk, rw_wv, rw_wo,
              rw_w0, rw_w1, rw_w2, rw_a0, rw_a1, rw_a2, rw_g1, rw_g2, rw_kk, rw_ka, rw_rk,
              rw_lnx_g, rw_lnx_b, at_wqkv, at_wo, ff_wup, ff_conv_w, ff_conv_b, ff_wdown):
    rw = (rw_mu, rw_wr, rw_wk, rw_wv, rw_wo, rw_w0, rw_w1, rw_w2, rw_a0, rw_a1, rw_a2,
          rw_g1, rw_g2, rw_kk, rw_ka, rw_rk, rw_lnx_g, rw_lnx_b)
    ff = (ff_wup, ff_conv_w, ff_conv_b, ff_wdown)
    dt = x_prompt.dtype
    bp, tp = x_prompt.shape[0], x_prompt.shape[1]
    ts = x_sample.shape[1]
    pos_p = jnp.arange(tp, dtype=jnp.int32)
    y_prompt, p_shift, p_wkv, p_kv, p_conv = run_trunk(
        x_prompt, pos_p,
        jnp.zeros((N_A, bp, D_MODEL), dt),
        jnp.zeros((N_A, bp, RW_HEADS, RW_HEAD, RW_HEAD), dt),
        None,
        jnp.zeros((DEPTH, bp, CONV_W - 1, 2 * D_FF), dt),
        norm_g, rw, at_wqkv, at_wo, ff)
    pos_s = PAST_LEN + jnp.arange(ts, dtype=jnp.int32)
    y_sample, s_shift, s_wkv, s_kv, s_conv = run_trunk(
        x_sample, pos_s, state_shift, state_wkv,
        (cache_kv_w128, cache_kv_w512, cache_kv_w2048), state_conv,
        norm_g, rw, at_wqkv, at_wo, ff)
    return (y_prompt, y_sample, p_shift, p_wkv, p_kv[0], p_kv[1], p_kv[2], p_conv,
            s_shift, s_wkv, s_kv[0], s_kv[1], s_kv[2], s_conv)


_drawn_inputs = setup_inputs


def setup_inputs(seed=0):
    import zlib

    import numpy as np

    out = dict(_drawn_inputs(seed))
    spreads = {}
    factors = {}
    for name, (base, spread) in spreads.items():
        noise = np.random.default_rng([zlib.crc32(name.encode()), seed]).standard_normal(out[name].shape)
        drawn = base * np.exp(spread * noise) if base else spread * noise
        out[name] = __import__('jax').numpy.asarray(drawn.astype(out[name].dtype))
    for name, factor in factors.items():
        out[name] = (out[name] * factor).astype(out[name].dtype)
    return out
```

```python
from contextlib import ExitStack

import numpy as np
import concourse.bass as bass
from concourse import mybir

F32 = mybir.dt.float32
ACT = mybir.ActivationFunctionType
ALU = mybir.AluOpType
AX = mybir.AxisListType

D, SEQ, NB, NS = 1024, 1024, 8, 8
P = 128
KT = D // P
T = SEQ + NB * NS
DFF = 2816
FT = DFF // P
PAIRS, HD, C = D // 128, 64, 64
NCH = T // C
GROUPS3 = ((128, 1), (512, 4), (2048, 16))
AP_ = 4
EPS, GN_EPS = 1e-6, 64e-5
DEC = float(np.exp(-0.5))
SCALE = HD ** -0.5
NEG = -1e30
TB = [(0, 384), (384, 384), (768, 320)]


class Machine:

    def __init__(self, nc, ctx):
        self.nc = nc
        sb = lambda n, w: ctx.enter_context(nc.sbuf_tensor("sb_" + n, [P, w], F32))
        self.x = sb("x", KT * T)
        self.h = sb("h", KT * T)
        self.big = sb("big", FT * T)
        self.w = sb("w", 5632)
        self.tmp = sb("tmp", 5216)
        self.ng = sb("gains", 2 * 4 * KT)
        self.ident = sb("ident", P)
        self.ones = sb("ones", P)
        self.eps = sb("eps", 2)
        self.ps = ctx.enter_context(nc.psum_tensor("ps", [P, 8, 512], F32))
        self.norm_sems = [ctx.enter_context(nc.semaphore(f"norm_{n}")) for n in (
            "squared", "summed", "rooted", "inverted", "scaled", "xin")]
        self.norms = 0
        self.X = self.x[:, :].rearrange("p (k t) -> p k t", t=T)
        self.H = self.h[:, :].rearrange("p (k t) -> p k t", t=T)


def tiles(region, start, count, width):
    return region[:, start:start + count * width].rearrange("p (n w) -> p n w", w=width)


def load_constants(m, a):
    nc = m.nc
    with ExitStack() as ctx:
        loaded = ctx.enter_context(nc.semaphore("const_loaded"))
        block = ctx.enter_context(nc.Block())

        @block.vector
        def _(dve):
            dve.memset(m.eps[:, 0:1], EPS)
            dve.memset(m.eps[:, 1:2], GN_EPS)

        @block.sync
        def _(sp):
            sp.dma_start(m.X, a["xT"]).then_inc(loaded, 16)
            sp.dma_start(m.ng[:, :], a["ng"]).then_inc(loaded, 16)
            sp.dma_start(m.ident[:, :], a["c_ident"]).then_inc(loaded, 16)
            sp.dma_start(m.ones[:, :], a["c_ones"]).then_inc(loaded, 16)
            sp.wait_ge(loaded, 64)


def rmsnorm(m, gain, src, add=False, reload=None):
    nc = m.nc
    squared, summed, rooted, inverted, scaled, xin = m.norm_sems
    u = m.norms
    m.norms += 1
    with ExitStack() as ctx:
        block = ctx.enter_context(nc.Block())
        sq = tiles(m.tmp, 0, 2, T)
        rs = tiles(m.tmp, 2 * T, 2, T)

        @block.sync
        def _(sp):
            if reload is not None:
                sp.dma_start(m.X, reload).then_inc(xin, 16)

        @block.scalar
        def _(act):
            for k in range(KT):
                if k >= 2:
                    act.wait_ge(summed, KT * u + k - 1)
                act.activation(sq[:, k % 2, :], src[:, k, :], ACT.Square).then_inc(squared, 1)
            act.wait_ge(summed, KT * u + KT)
            for b, (t0, n) in enumerate(TB):
                act.activation(rs[:, 0, t0:t0 + n], m.ps[:, b, 0:n], ACT.Sqrt,
                               bias=m.eps[:, 0:1], scale=1.0 / D).then_inc(rooted, 1)

        @block.tensor
        def _(pe):
            for k in range(KT):
                pe.wait_ge(squared, KT * u + k + 1)
                for b, (t0, n) in enumerate(TB):
                    mm = pe.matmul(m.ps[:, b, 0:n], m.ones[:, :], sq[:, k % 2, t0:t0 + n],
                                   start=(k == 0), stop=(k == KT - 1))
                mm.then_inc(summed, 1)

        @block.vector
        def _(dve):
            for b, (t0, n) in enumerate(TB):
                dve.wait_ge(rooted, 3 * u + b + 1)
                dve.reciprocal(rs[:, 1, t0:t0 + n], rs[:, 0, t0:t0 + n]).then_inc(inverted, 1)
            dve.wait_ge(inverted, 3 * u + 3)
            for k in range(KT):
                g = m.ng[:, gain * KT + k:gain * KT + k + 1]
                dve.scalar_tensor_tensor(out=m.H[:, k, :], in0=src[:, k, :], scalar=g, in1=rs[:, 1, :],
                                         op0=ALU.mult, op1=ALU.mult).then_inc(scaled, 1)

        @block.gpsimd
        def _(pool):
            if add:
                if reload is not None:
                    pool.wait_ge(xin, 16)
                for k in range(KT):
                    pool.wait_ge(scaled, KT * u + k + 1)
                    pool.tensor_tensor(m.X[:, k, :], m.X[:, k, :], m.H[:, k, :], ALU.add)


def ffn(m, a, layer):
    nc = m.nc
    PADW = SEQ + 2 + NB * (NS + 2)
    with ExitStack() as ctx:
        sem = lambda n: ctx.enter_context(nc.semaphore(f"ff{layer}_{n}"))
        wload = [sem(f"wload{i}") for i in range(2)]
        up, padded, conv, gelu, hidden, kept = (
            sem(n) for n in ("up", "padded", "conv", "gelu", "hidden", "kept"))
        stored = [sem(f"stored{i}") for i in range(2)]
        wd = [sem(f"wd{i}") for i in range(2)]
        down, out = sem("down"), sem("out")
        hid = tiles(m.big, 0, FT, T)
        wt = [[tiles(m.w, (2 * s + q) * D, KT, P) for q in range(2)] for s in range(2)]
        hp = tiles(m.tmp, 0, 4, PADW)
        cval = m.w[:, 4 * D:4 * D + T]
        vec = tiles(m.tmp, 4 * PADW, 2, 40)
        last2 = tiles(m.tmp, 4 * PADW + 80, 4, 18)
        sview = lambda ap: ap[:, SEQ:T].rearrange("p (b s) -> p b s", b=NB)
        pview = lambda ap: ap[:, SEQ + 2:PADW].rearrange("p (b s) -> p b s", b=NB)
        block = ctx.enter_context(nc.Block())

        @block.sync
        def _(sp):
            def keep_rows(tile, s):
                sp.wait_ge(kept, tile * 2 + 2)
                for q in range(2):
                    sp.dma_start(a["o_conv"][layer, bass.ds(tile + q * FT, 1)].rearrange("a p c -> p (a c)"),
                                 last2[:, 2 * s + q, :]).then_inc(stored[s], 16)

            for s in range(2):
                for q in range(2):
                    sp.dma_start(wt[s][q], a["wup"][layer, q * FT + s]).then_inc(wload[s], 16)
                sp.dma_start(vec[:, s, :], a["ffv"][layer, s]).then_inc(wload[s], 16)
            with sp.Fori(1, FT // 2) as i:
                for s in range(2):
                    sp.wait_ge(up, i * 12 - 12 + 6 * s + 6)
                    for q in range(2):
                        sp.dma_start(wt[s][q], a["wup"][layer, bass.ds(i * 2 + (q * FT + s), 1)].rearrange(
                            "a p k c -> p (a k) c")).then_inc(wload[s], 16)
                    keep_rows(i * 2 + s - 2, s)
                    sp.wait_ge(hidden, i * 2 + s - 1)
                    sp.dma_start(vec[:, s, :], a["ffv"][layer, bass.ds(i * 2 + s, 1)].rearrange(
                        "a p k -> p (a k)")).then_inc(wload[s], 16)
            for s in range(2):
                keep_rows(FT - 2 + s, s)
                sp.wait_ge(stored[s], FT * 16)
            sp.wait_ge(up, FT * 6)
            sp.wait_ge(hidden, FT)
            wdt = [tiles(m.w, s * DFF, FT, P) for s in range(2)]
            for s in range(2):
                sp.dma_start(wdt[s], a["wdown"][layer, s]).then_inc(wd[s], 16)
            with sp.Fori(1, KT // 2) as i:
                for s in range(2):
                    sp.wait_ge(down, i * 6 - 6 + 3 * s + 3)
                    sp.dma_start(wdt[s], a["wdown"][layer, bass.ds(i * 2 + s, 1)].rearrange(
                        "a p k c -> p (a k) c")).then_inc(wd[s], 16)

        @block.tensor
        def _(pe):
            with pe.Fori(0, FT // 2) as i:
                for s in range(2):
                    pe.wait_ge(wload[s], i * 48 + 48)
                    for q in range(2):
                        for b, (t0, n) in enumerate(TB):
                            u = 6 * s + 3 * q + b
                            pe.wait_ge(padded, i * 12 + u + 1)
                            for k in range(KT):
                                mm = pe.matmul(m.ps[:, 3 * q + b, 0:n], wt[s][q][:, k, :], m.H[:, k, t0:t0 + n],
                                               start=(k == 0), stop=(k == KT - 1))
                            mm.then_inc(up, 1)
            wdt = [tiles(m.w, s * DFF, FT, P) for s in range(2)]
            pe.wait_ge(hidden, FT)
            with pe.Fori(0, KT // 2) as i:
                for s in range(2):
                    pe.wait_ge(wd[s], i * 16 + 16)
                    for b, (t0, n) in enumerate(TB):
                        pe.wait_ge(out, i * 6 + 3 * s + b + 1)
                        for k in range(FT):
                            mm = pe.matmul(m.ps[:, 3 * s + b, 0:n], wdt[s][:, k, :], hid[:, k, t0:t0 + n],
                                           start=(k == 0), stop=(k == FT - 1))
                        mm.then_inc(down, 1)

        @block.scalar
        def _(act):
            for _u in range(6):
                act.nop().then_inc(padded, 1)
                act.nop().then_inc(out, 1)
            for s in range(4):
                act.activation(hp[:, s, 0:2], m.ident[:, 0:2], ACT.Copy, scale=0.0)
            with act.Fori(0, FT // 2) as i:
                for s in range(2):
                    act.wait_ge(wload[s], i * 48 + 48)
                    act.wait_ge(conv, i * 4 + 2 * s + 1)
                    for q in range(2):
                        row = hp[:, 2 * s + q, :]
                        act.activation(pview(row)[:, :, 0:2],
                                       vec[:, s, 8 + 16 * q:24 + 16 * q].rearrange("p (b s) -> p b s", b=NB), ACT.Copy)
                        for b, (t0, n) in enumerate(TB):
                            act.wait_ge(up, i * 12 + 6 * s + 3 * q + b + 1)
                            src = m.ps[:, 3 * q + b, 0:n]
                            if b < 2:
                                act.activation(row[:, 2 + t0:2 + t0 + n], src, ACT.Copy).then_inc(padded, 1)
                            else:
                                act.activation(row[:, 2 + t0:2 + SEQ], src[:, 0:SEQ - t0], ACT.Copy)
                                act.activation(pview(row)[:, :, 2:2 + NS],
                                               src[:, SEQ - t0:n].rearrange("p (b s) -> p b s", b=NB),
                                               ACT.Copy).then_inc(padded, 1)
                    act.wait_ge(conv, i * 4 + 2 * s + 4)
                    gate = hid[:, bass.ds(i * 2 + s, 1), :].rearrange("p a t -> p (a t)")
                    act.activation(gate, gate, ACT.Gelu_apprx_tanh).then_inc(gelu, 1)
            with act.Fori(0, KT // 2) as i:
                for s in range(2):
                    for b, (t0, n) in enumerate(TB):
                        act.wait_ge(down, i * 6 + 3 * s + b + 1)
                        act.activation(m.H[:, bass.ds(i * 2 + s, 1), t0:t0 + n].rearrange("p a t -> p (a t)"),
                                       m.ps[:, 3 * s + b, 0:n], ACT.Copy).then_inc(out, 1)

        @block.vector
        def _(dve):
            for _u in range(3):
                dve.nop().then_inc(conv, 1)
            with dve.Fori(0, FT // 2) as i:
                for s in range(2):
                    gate = hid[:, bass.ds(i * 2 + s, 1), :].rearrange("p a t -> p (a t)")
                    dve.wait_ge(wload[s], i * 48 + 48)
                    for q, dst in enumerate((gate, cval)):
                        row = hp[:, 2 * s + q, :]
                        dve.wait_ge(padded, i * 12 + 6 * s + 3 * q + 3 + 6)
                        keep = last2[:, 2 * s + q, :]
                        dve.tensor_copy(keep[:, 0:2], row[:, SEQ:SEQ + 2])
                        dve.tensor_copy(keep[:, 2:18].rearrange("p (b s) -> p b s", b=NB),
                                        pview(row)[:, :, NS:NS + 2]).then_inc(kept, 1)
                        for part_out, part_in in ((dst[:, 0:SEQ], lambda j: row[:, j:j + SEQ]),
                                                  (sview(dst), lambda j: pview(row)[:, :, j:j + NS])):
                            cw = lambda j: vec[:, s, 4 * q + j:4 * q + j + 1]
                            dve.tensor_scalar(part_out, part_in(0), cw(0), cw(3), ALU.mult, ALU.add)
                            for j in (1, 2):
                                dve.drain()
                                last = dve.scalar_tensor_tensor(out=part_out, in0=part_in(j), scalar=cw(j),
                                                                in1=part_out, op0=ALU.mult, op1=ALU.add)
                        last.then_inc(conv, 1)
                    dve.wait_ge(gelu, i * 2 + s + 1)
                    dve.wait_ge(conv, i * 4 + 2 * s + 5)
                    dve.tensor_tensor(gate, gate, cval, ALU.mult).then_inc(hidden, 1)
                    dve.wait_ge(hidden, i * 2 + s + 1)
                    dve.wait_ge(stored[s], i * 32 + 32)


def dense(m, name, w, kt, rhs, out):
    nc = m.nc
    with ExitStack() as ctx:
        sem = lambda n: ctx.enter_context(nc.semaphore(f"{name}_{n}"))
        wload = [sem(f"wload{i}") for i in range(2)]
        product, copied = sem("product"), sem("copied")
        wt = [tiles(m.w, s * kt * P, kt, P) for s in range(2)]
        block = ctx.enter_context(nc.Block())

        @block.sync
        def _(sp):
            for s in range(2):
                sp.dma_start(wt[s], w[s]).then_inc(wload[s], 16)
            with sp.Fori(1, KT // 2) as i:
                for s in range(2):
                    sp.wait_ge(product, i * 6 - 6 + 3 * s + 3)
                    sp.dma_start(wt[s], w[bass.ds(i * 2 + s, 1)].rearrange(
                        "a p k c -> p (a k) c")).then_inc(wload[s], 16)

        @block.tensor
        def _(pe):
            with pe.Fori(0, KT // 2) as i:
                for s in range(2):
                    pe.wait_ge(wload[s], i * 16 + 16)
                    for b, (t0, n) in enumerate(TB):
                        pe.wait_ge(copied, i * 6 + 3 * s + b + 1)
                        for k in range(kt):
                            mm = pe.matmul(m.ps[:, 3 * s + b, 0:n], wt[s][:, k, :], rhs[:, k, t0:t0 + n],
                                           start=(k == 0), stop=(k == kt - 1))
                        mm.then_inc(product, 1)

        @block.scalar
        def _(act):
            for _u in range(6):
                act.nop().then_inc(copied, 1)
            with act.Fori(0, KT // 2) as i:
                for s in range(2):
                    for b, (t0, n) in enumerate(TB):
                        act.wait_ge(product, i * 6 + 3 * s + b + 1)
                        act.activation(out[:, bass.ds(i * 2 + s, 1), t0:t0 + n].rearrange("p a t -> p (a t)"),
                                       m.ps[:, 3 * s + b, 0:n], ACT.Copy).then_inc(copied, 1)


def store_y(m, a):
    nc = m.nc
    with ExitStack() as ctx:
        stored = ctx.enter_context(nc.semaphore("y_stored"))
        block = ctx.enter_context(nc.Block())

        @block.sync
        def _(sp):
            sp.dma_start(a["o_y"], m.X).then_inc(stored, 16)
            sp.wait_ge(stored, 16)
def rwkv_inputs(m, a, scratch):
    nc = m.nc
    L1 = 64 + 64 + 160
    MIXES = (("w", 1), ("a", 4), ("g", 5), ("r", 0), ("k", 2), ("v", 3))
    NU = 3 * PAIRS
    with ExitStack() as ctx:
        sem = lambda n: ctx.enter_context(nc.semaphore(f"in_{n}"))
        params, shifted, mixed, product, copied, kept, rows_out = (
            sem(n) for n in ("params", "shifted", "mixed", "product", "copied", "kept", "rows_out"))
        wload = [sem(f"wload{i}") for i in range(2)]
        landed = [sem(f"landed{i}") for i in range(2)]
        xx = tiles(m.big, 0, KT, T)
        mix = [tiles(m.x, 0, KT, T), tiles(m.big, KT * T, KT, T)]
        lora = tiles(m.big, 16 * T, 3, T)
        wt = [tiles(m.w, s * D, KT, P) for s in range(2)]
        stage = tiles(m.w, 2 * D, 2, T)
        l1 = tiles(m.tmp, 0, KT, L1)
        mu = tiles(m.tmp, KT * L1, 6, KT)
        prev = tiles(m.tmp, KT * L1 + 48, KT, NB)
        last = tiles(m.tmp, KT * L1 + 112, KT, 1 + NB)
        block = ctx.enter_context(nc.Block())

        @block.sync
        def _(sp):
            sp.dma_start(mu, a["mu"]).then_inc(params, 16)
            sp.dma_start(prev, a["shiftT"]).then_inc(params, 16)
            sp.dma_start(l1, a["lw1"]).then_inc(params, 16)
            for s in range(2):
                sp.dma_start(wt[s], a["wrkv"][s]).then_inc(wload[s], 16)
            sp.wait_ge(kept, 1)
            sp.dma_start(a["o_shift"], last).then_inc(rows_out, 16)
            with sp.Fori(1, NU // 2) as i:
                for s in range(2):
                    sp.wait_ge(copied, i * 6 + 3 * s + 9)
                    sp.dma_start(scratch[bass.ds(i * 2 + s - 2, 1)].rearrange("a p t -> p (a t)"),
                                 stage[:, s, :]).then_inc(landed[s], 16)
                    sp.wait_ge(landed[s], i * 16)
                    sp.dma_start(wt[s], a["wrkv"][bass.ds(i * 2 + s, 1)].rearrange(
                        "a p k c -> p (a k) c")).then_inc(wload[s], 16)
            for s in range(2):
                sp.wait_ge(copied, NU * 3 + 3 * s + 9)
                sp.dma_start(scratch[NU - 2 + s], stage[:, s, :]).then_inc(landed[s], 16)
            for s in range(2):
                sp.wait_ge(landed[s], NU * 8)
            sp.wait_ge(rows_out, 16)

        @block.gpsimd
        def _(pool):
            pool.tensor_copy(last, m.H[:, :, SEQ - 1:T:NS]).then_inc(kept, 1)

        @block.vector
        def _(dve):
            dve.wait_ge(params, 48)
            dve.tensor_tensor(xx[:, :, 1:SEQ], m.H[:, :, 0:SEQ - 1], m.H[:, :, 1:SEQ], ALU.subtract)
            dve.tensor_scalar(xx[:, :, 0:1], m.H[:, :, 0:1], -1.0, None, ALU.mult)
            for k in range(KT):
                hs = m.H[:, k, SEQ:T].rearrange("p (b s) -> p b s", b=NB)
                xs = xx[:, k, SEQ:T].rearrange("p (b s) -> p b s", b=NB)
                dve.tensor_tensor(xs[:, :, 1:NS], hs[:, :, 0:NS - 1], hs[:, :, 1:NS], ALU.subtract)
                ins = dve.tensor_tensor(xs[:, :, 0], prev[:, k, :], hs[:, :, 0], ALU.subtract)
            ins.then_inc(shifted, 1)
            dve.wait_ge(shifted, 1)
            for j, (_n, row) in enumerate(MIXES):
                for k in range(KT):
                    if j >= 2:
                        dve.wait_ge(product, (3, 6, 12, 12 + 24, 12 + 48)[j - 2])
                    dve.scalar_tensor_tensor(out=mix[j % 2][:, k, :], in0=xx[:, k, :], scalar=mu[:, row, k:k + 1],
                                             in1=m.H[:, k, :], op0=ALU.mult, op1=ALU.add).then_inc(mixed, 1)

        @block.tensor
        def _(pe):
            u = 0
            for j, cols in enumerate(((0, 64), (64, 128), (128, 256), (256, 288))):
                src = (0, 1, 0, 0)[j]
                lo = 64 if j == 1 else 0
                if j == 0:
                    pe.wait_ge(params, 48)
                for b, (t0, n) in enumerate(TB):
                    if j >= 2:
                        pe.wait_ge(copied, 3 * (j - 2) + b + 1)
                    for k in range(KT):
                        if b == 0 and j < 3:
                            pe.wait_ge(mixed, 8 * j + k + 1)
                        mm = pe.matmul(m.ps[lo:lo + cols[1] - cols[0], 3 * (j % 2) + b, 0:n],
                                       l1[:, k, cols[0]:cols[1]], mix[src][:, k, t0:t0 + n],
                                       start=(k == 0), stop=(k == KT - 1))
                    mm.then_inc(product, 1)
            for j in range(3):
                with pe.Fori(0, PAIRS // 2) as i:
                    for s in range(2):
                        pe.wait_ge(wload[s], i * 16 + (16 + 64 * j))
                        pe.wait_ge(mixed, 32 + 8 * j)
                        for b, (t0, n) in enumerate(TB):
                            pe.wait_ge(copied, i * 6 + (24 * j + 3 * s + 6 + b + 1))
                            for k in range(KT):
                                mm = pe.matmul(m.ps[:, 3 * s + b, 0:n], wt[s][:, k, :],
                                               mix[(j + 1) % 2][:, k, t0:t0 + n],
                                               start=(k == 0), stop=(k == KT - 1))
                            mm.then_inc(product, 1)

        @block.scalar
        def _(act):
            for j, (tile, lo, rows, func) in enumerate(((0, 0, 64, ACT.Tanh), (0, 64, 64, ACT.Copy),
                                                        (1, 0, 128, ACT.Sigmoid), (2, 0, 32, ACT.Sigmoid))):
                for b, (t0, n) in enumerate(TB):
                    act.wait_ge(product, 3 * j + b + 1)
                    act.activation(lora[lo:lo + rows, tile, t0:t0 + n], m.ps[lo:lo + rows, 3 * (j % 2) + b, 0:n],
                                   func).then_inc(copied, 1)
            with act.Fori(0, NU // 2) as i:
                for s in range(2):
                    for b, (t0, n) in enumerate(TB):
                        act.wait_ge(product, i * 6 + (12 + 3 * s + b + 1))
                        act.activation(stage[:, s, t0:t0 + n], m.ps[:, 3 * s + b, 0:n], ACT.Copy).then_inc(copied, 1)


def rwkv_core(m, a, scratch):
    nc = m.nc
    G3 = [(0, 6), (6, 12), (12, NCH)]
    PC = NCH - 1
    SC = NCH - 1
    with ExitStack() as ctx:
        sem = lambda n: ctx.enter_context(nc.semaphore(f"rw_{n}"))
        consts, zeroed, loaded, prep_d, prep_a, bdin, copies, full, outd, outa, am, tb, yb, sb2, ub, stp, std, masked, out_s, done = (
            sem(n) for n in ("consts", "zeroed", "loaded", "prep_d", "prep_a", "bdin", "copies", "psum_full", "dve_out",
                             "act_out", "level_mask", "t_bd", "y_bd", "s_bd", "u_bd", "state_psum", "state", "batch_masked",
                             "state_out", "pair_done"))
        bdt = lambda reg, st: reg[:, st:st + NCH * P].rearrange("p (c j) -> p c j", j=P)
        bd = [bdt(m.x, s * 2 * T) for s in range(4)] + [bdt(m.big, s * 2 * T) for s in range(5)]
        flat = [m.big[:, (10 + s) * T:(11 + s) * T] for s in range(6)] + \
               [m.big[:, (19 + s) * T:(20 + s) * T] for s in range(3)] + \
               [m.w[:, s * T:(s + 1) * T] for s in range(5)]
        lora = tiles(m.big, 16 * T, 3, T)
        offs = {"tmp": 0}

        def small(w):
            o = offs["tmp"]
            offs["tmp"] += w
            assert offs["tmp"] <= 5216
            return m.tmp[:, o:o + w]

        reset = small(T)
        lm = small(6 * P).rearrange("p (l j) -> p l j", l=6)
        ms = small(4 * C).rearrange("p (l j) -> p l j", l=4)
        two, bones = small(C), small(P)
        zeros, mean64 = m.w[:, 5 * T:5 * T + HD], m.w[:, 5 * T + HD:5 * T + HD + P]
        rowb = small(NB)
        lw2 = small(4 * P).rearrange("p (n j) -> p n j", n=4)
        pv = small(8)
        pend = small(PC + NB)
        qm = small(NB * (P + NS))
        sout = small(9 * HD).rearrange("p (n v) -> p n v", n=9)
        sbc = small(NB * HD).rearrange("p (b v) -> p b v", b=NB)
        V, G, RKR, Rt, Qt, Kk, SG, A, LS, EP, EI, Xs, Ts = flat[:13]
        sbb = flat[13][:, 0:NB * P].rearrange("p (b j) -> p b j", b=NB)
        Bb, Kb, Vb, Qb, ATb, KQb, BTb, KTb, VTb = bd
        AMb, TBb, Yb, Hb, Eb, Sb, Ub = bd[0], bd[1], bd[2], bd[0], bd[1], bd[4], bd[5]
        ch = lambda t: t.rearrange("p (c s) -> p c s", s=C)
        RBc, RKc, Btc, Vc, Qtc, BVc, Xc, Yc, Tc = (ch(t) for t in (Kk, SG, A, LS, EP, EI, Xs, Qt, Ts))
        Gc, Nc, Sc, Wc, Uc = Xc, Qtc, Tc, Btc, Yc
        YT, YC, SQ2, RS2, BB = EI, Xs, EP, A, Ts
        um, vm = Kk[:, 0:NB * HD].rearrange("p (b v) -> p b v", b=NB), SG[:, 0:NB * HD].rearrange("p (b v) -> p b v", b=NB)
        Qch, Rch = ch(Qt), ch(Rt)
        PW0, PA0, PKK, PKA, PRK, PLG, PLB = range(7)
        col = lambda j: pv[:, j:j + 1]
        bc = lambda ap, n: ap.unsqueeze(1).broadcast_to([ap.shape[0], n, ap.shape[1]])
        halves = ((0, 64), (64, 128))

        def bank(st, g, lo=0, hi=P, c0=0, c1=None):
            n = G3[g][1] - G3[g][0] if c1 is None else c1
            return m.ps[lo:hi, 3 * (st % 2) + g, c0 * C:n * C].rearrange("p (c s) -> p c s", s=C)

        TAKER = {"sig": "a", "a": "a", "g": "a", "kn": "d", "at": "d", "kq": "d", "rb": "d", "rk": "d", "bt": "a",
                 "kt": "a", "vt": "a", "qt": "a", "bv": "a", "t0": "d"}
        for l in range(1, 6):
            TAKER[f"t{l}"] = "d"
            if l < 5:
                TAKER[f"x{l}"] = "d"
            TAKER[f"y{l}"] = "d"
        TAKER |= {"G": "a", "H": "d", "E": "d", "N": "d", "W": "d", "U": "a", "Y": "a", "mean": "d", "var": "a", "bonus": "d"}
        ORDER = list(TAKER)
        NST = len(ORDER)
        idx = {s: n for n, s in enumerate(ORDER)}
        nd = sum(v == "d" for v in TAKER.values()) * 3
        na = sum(v == "a" for v in TAKER.values()) * 3

        def taken(st, g):
            who = TAKER[st]
            return 3 * sum(TAKER[x] == who for x in ORDER[:idx[st]]) + g + 1

        def wait_full(eng, i, st, g):
            eng.wait_ge(full, i * (3 * NST) + (3 * idx[st] + g + 1))

        def wait_taken(eng, i, st, g):
            sem, count = (outd, i * nd + taken(st, g)) if TAKER[st] == "d" else (outa, i * na + taken(st, g))
            eng.wait_ge(sem, count)

        block = ctx.enter_context(nc.Block())

        @block.sync
        def _(sp):
            for t, n in ((reset, "c_reset"), (lm, "c_level"), (ms, "c_masks"), (two, "c_two"), (bones, "c_bones"),
                         (mean64, "c_mean64"), (rowb, "c_rowb")):
                sp.dma_start(t, a[n]).then_inc(consts, 16)
            with sp.Fori(0, PAIRS) as i:
                sp.wait_ge(done, i * 1 + 1)
                for t, n in ((Rt, 0), (Kk, PAIRS), (V, 2 * PAIRS)):
                    sp.dma_start(t, scratch[bass.ds(i + n, 1)].rearrange("a p t -> p (a t)")).then_inc(loaded, 16)
                sp.dma_start(lw2, a["lw2"][bass.ds(i, 1)].rearrange("a p n j -> p (a n) j")).then_inc(loaded, 16)
                sp.dma_start(pv, a["pv"][bass.ds(i, 1)].rearrange("a p n -> p (a n)")).then_inc(loaded, 16)
                sp.dma_start(sbc, a["s0c"][bass.ds(i, 1)].rearrange("a p b v -> p (a b) v")).then_inc(loaded, 16)
                sp.dma_start(sbb, a["s0bd"][bass.ds(i, 1)].rearrange("a p b v -> p (a b) v")).then_inc(loaded, 16)
                sp.wait_ge(std, i * 17 + 17)
                sp.dma_start(a["o_state"][bass.ds(i, 1)].rearrange("a p n v -> p (a n) v"), sout).then_inc(out_s, 16)
            sp.wait_ge(out_s, 16 * PAIRS)

        @block.gpsimd
        def _(pool):
            for t in bd:
                pool.memset(t, 0.0)
            pool.memset(zeros, 0.0)
            pool.memset(qm, 0.0).then_inc(zeroed, 1)
            pool.wait_ge(zeroed, 1)
            pool.wait_ge(consts, 7 * 16)
            with pool.Fori(0, PAIRS) as i:
                for l in range(6):
                    for g, (c0, c1) in enumerate(G3):
                        if l == 0:
                            wait_taken(pool, i, "at", g)
                            wait_full(pool, i, "bt", g)
                        else:
                            wait_full(pool, i, f"t{l - 1}", g)
                            if l == 1:
                                wait_taken(pool, i, "t0", g)
                        pool.tensor_tensor(AMb[:, c0:c1, :], ATb[:, c0:c1, :], bc(lm[:, l, :], c1 - c0),
                                           ALU.mult).then_inc(am, 1)
                wait_taken(pool, i, "U", 2)
                wait_full(pool, i, "Y", 2)
                pool.tensor_tensor(um, bc(Uc[:, SC, :], NB), rowb.unsqueeze(2).broadcast_to([P, NB, HD]), ALU.mult)
                pool.tensor_tensor(vm, bc(Vc[:, SC, :], NB), rowb.unsqueeze(2).broadcast_to([P, NB, HD]),
                                   ALU.mult).then_inc(masked, 1)

        @block.scalar
        def _(act):
            with act.Fori(0, PAIRS) as i:
                act.wait_ge(loaded, i * 112 + 112)
                for st, dst, func, bias in (("sig", SG, ACT.Sigmoid, PW0), ("a", A, ACT.Sigmoid, PA0), ("g", G, ACT.Copy, None)):
                    for g, (t0, n) in enumerate(TB):
                        wait_full(act, i, st, g)
                        src = m.ps[:, 3 * (idx[st] % 2) + g, 0:n]
                        if bias is None:
                            act.activation(dst[:, t0:t0 + n], src, func).then_inc(outa, 1)
                        else:
                            act.activation(dst[:, t0:t0 + n], src, func, bias=col(bias)).then_inc(outa, 1)
                act.wait_ge(prep_d, i * 7 + 1)
                act.activation(EP, Qt, ACT.Square).then_inc(prep_a, 1)
                wait_taken(act, i, "kn", 2)
                act.activation(EI, EI, ACT.Sqrt).then_inc(prep_a, 1)
                act.wait_ge(prep_d, i * 7 + 4)
                act.activation(EP, LS, ACT.Exp, scale=-DEC).then_inc(prep_a, 1)
                act.activation(EI, LS, ACT.Exp, scale=DEC).then_inc(prep_a, 1)
                act.activation(SG, SG, ACT.Exp, scale=-DEC).then_inc(prep_a, 1)
                act.drain()
                act.activation(pend[:, 0:PC], EP[:, C - 1:SEQ:C], ACT.Copy)
                act.activation(pend[:, PC:PC + NB], EP[:, SEQ + NS - 1:T:NS], ACT.Copy).then_inc(prep_a, 1)

                for lo, hi in halves:
                    act.activation(Vb[lo:hi, :, lo:hi], ch(V)[lo:hi], ACT.Copy)
                act.wait_ge(prep_d, i * 7 + 7)
                for lo, hi in halves:
                    act.activation(Qb[lo:hi, :, lo:hi], Qch[lo:hi], ACT.Copy)
                    dst = qm[lo:hi].rearrange("p (b x) -> p b x", x=P + NS)[:, :, lo:lo + NS]
                    ins = act.activation(dst, Qt[lo:hi, SEQ:T].rearrange("p (b s) -> p b s", b=NB), ACT.Copy)
                ins.then_inc(copies, 1)

                def out(st, compact, bdst, scale=1.0):
                    for g, (c0, c1) in enumerate(G3):
                        wait_full(act, i, st, g)
                        if compact is not None:
                            ins = act.activation(compact[:, c0:c1, :], bank(idx[st], g), ACT.Copy, scale=scale)
                        if bdst is not None:
                            for lo, hi in halves:
                                ins = act.activation(bdst[lo:hi, c0:c1, lo:hi], bank(idx[st], g, lo, hi), ACT.Copy)
                        ins.then_inc(outa, 1)

                out("bt", Btc, BTb)
                out("kt", None, KTb)
                out("vt", Vc, VTb)
                out("qt", Qtc, None)
                out("bv", BVc, None)
                for g, (c0, c1) in enumerate(G3):
                    wait_taken(act, i, "t0", g)
                    for lo, hi in halves:
                        ins = act.activation(Yb[lo:hi, c0:c1, lo:hi], Yc[lo:hi, c0:c1, :], ACT.Copy)
                    ins.then_inc(yb, 1)
                for l in range(1, 6):
                    for g, (c0, c1) in enumerate(G3):
                        wait_taken(act, i, f"t{l}", g)
                        for lo, hi in halves:
                            ins = act.activation(TBb[lo:hi, c0:c1, lo:hi], Tc[lo:hi, c0:c1, :], ACT.Copy)
                        ins.then_inc(tb, 1)
                    for g, (c0, c1) in enumerate(G3):
                        wait_taken(act, i, f"y{l}", g)
                        for lo, hi in halves:
                            ins = act.activation(Yb[lo:hi, c0:c1, lo:hi], Yc[lo:hi, c0:c1, :], ACT.Copy)
                        ins.then_inc(yb, 1)
                out("G", Gc, None, scale=-1.0)
                for g, (c0, c1) in enumerate(G3):
                    act.wait_ge(std, i * 17 + min(c1, PC) - 1)
                    lo_c, hi_c = max(c0, 1), min(c1, PC)
                    for lo, hi in halves:
                        ins = act.activation(Sb[lo:hi, lo_c:hi_c, lo:hi], Sc[lo:hi, lo_c - 1:hi_c - 1, :], ACT.Copy)
                    ins.then_inc(sb2, 1)
                out("U", Uc, None, scale=-1.0)
                for g, (c0, c1) in enumerate(G3):
                    wait_taken(act, i, "U", g)
                    for lo, hi in halves:
                        ins = act.activation(Ub[lo:hi, c0:c1, lo:hi], Uc[lo:hi, c0:c1, :], ACT.Copy)
                    ins.then_inc(ub, 1)
                for g, (t0, n) in enumerate(TB):
                    wait_full(act, i, "Y", g)
                    act.activation(YT[:, t0:t0 + n], m.ps[:, 3 * (idx["Y"] % 2) + g, 0:n], ACT.Copy).then_inc(outa, 1)
                wait_taken(act, i, "mean", 2)
                act.activation(SQ2, YC, ACT.Square).then_inc(prep_a, 1)
                for g, (t0, n) in enumerate(TB):
                    wait_full(act, i, "var", g)
                    act.activation(RS2[:, t0:t0 + n], m.ps[:, 3 * (idx["var"] % 2) + g, 0:n], ACT.Sqrt,
                                   bias=m.eps[:, 1:2]).then_inc(outa, 1)

        @block.vector
        def _(dve):
            dve.nop().then_inc(done, 1)
            dve.wait_ge(zeroed, 1)
            dve.wait_ge(consts, 7 * 16)
            with dve.Fori(0, PAIRS) as i:
                dve.wait_ge(loaded, i * 112 + 112)
                dve.tensor_scalar(Qt, Kk, col(PKK), None, ALU.mult).then_inc(prep_d, 1)
                wait_taken(dve, i, "sig", 2)
                dve.tensor_tensor_scan(LS, reset, SG, 0.0, ALU.mult, ALU.add)
                dve.drain()
                dve.tensor_tensor(SG, LS, SG, ALU.subtract).then_inc(prep_d, 1)
                wait_taken(dve, i, "a", 2)
                dve.tensor_scalar(Ts, A, -1.0, col(PKA), ALU.add, ALU.mult)
                dve.drain()
                dve.scalar_tensor_tensor(out=Kk, in0=Ts, scalar=1.0, in1=Kk, op0=ALU.add, op1=ALU.mult)
                dve.drain()
                dve.scalar_tensor_tensor(out=RKR, in0=Rt, scalar=col(PRK), in1=Kk, op0=ALU.mult,
                                         op1=ALU.mult).then_inc(prep_d, 1)
                for g, (t0, n) in enumerate(TB):
                    wait_full(dve, i, "kn", g)
                    dve.tensor_scalar(EI[:, t0:t0 + n], m.ps[:, 3 * (idx["kn"] % 2) + g, 0:n], 1e-24, None,
                                      ALU.max).then_inc(outd, 1)
                dve.wait_ge(prep_a, i * 7 + 2)
                dve.reciprocal(Xs, EI)
                dve.drain()
                dve.tensor_tensor(Qt, Qt, Xs, ALU.mult).then_inc(prep_d, 1)
                dve.wait_ge(prep_d, i * 7 + 4)
                dve.tensor_tensor(A, A, Qt, ALU.mult).then_inc(prep_d, 1)
                dve.wait_ge(prep_a, i * 7 + 6)
                dve.wait_ge(prep_d, i * 7 + 5)
                dve.tensor_tensor(Rt, Rt, EP, ALU.mult).then_inc(prep_d, 1)
                dve.tensor_tensor(Qt, Qt, SG, ALU.mult).then_inc(prep_d, 1)
                for lo, hi in halves:
                    dve.tensor_tensor(Bb[lo:hi, :, lo:hi], ch(A)[lo:hi], ch(EI)[lo:hi], ALU.mult)
                    ins = dve.tensor_tensor(Kb[lo:hi, :, lo:hi], ch(Kk)[lo:hi], ch(EI)[lo:hi], ALU.mult)
                ins.then_inc(bdin, 1)

                def split(g):
                    c0, c1 = G3[g]
                    return [(c0, c1, 0)] if g < 2 else [(c0, PC, 0), (SC, SC + 1, 1)]

                for st, which, dst in (("at", 0, ATb), ("kq", 0, KQb), ("rb", 1, RBc), ("rk", 1, RKc)):
                    for g, (c0, c1) in enumerate(G3):
                        wait_full(dve, i, st, g)
                        for s0, s1, sampled in split(g):
                            mask = ms[:, which + 2 * sampled, :]
                            if which:
                                ins = dve.tensor_tensor(dst[:, s0:s1, :], bank(idx[st], g, 0, P, s0 - c0, s1 - c0),
                                                        bc(mask, s1 - s0), ALU.mult)
                            else:
                                for lo, hi in halves:
                                    ins = dve.tensor_tensor(dst[lo:hi, s0:s1, lo:hi],
                                                            bank(idx[st], g, lo, hi, s0 - c0, s1 - c0),
                                                            bc(mask[lo:hi], s1 - s0), ALU.mult)
                        ins.then_inc(outd, 1)
                dve.wait_ge(copies, i * 1 + 1)
                for g, (c0, c1) in enumerate(G3):
                    dve.wait_ge(am, i * 18 + g + 1)
                    dve.tensor_tensor(Yc[:, c0:c1, :], AMb[:, c0:c1, 0:C], AMb[:, c0:c1, C:P], ALU.add)
                    dve.drain()
                    dve.tensor_tensor(Yc[:, c0:c1, :], bc(two, c1 - c0), Yc[:, c0:c1, :], ALU.subtract)
                    wait_full(dve, i, "t0", g)
                    dve.tensor_tensor(Xc[:, c0:c1, :], bc(two, c1 - c0), bank(idx["t0"], g), ALU.subtract).then_inc(outd, 1)
                for l in range(1, 6):
                    for g, (c0, c1) in enumerate(G3):
                        wait_full(dve, i, f"t{l}", g)
                        dve.tensor_copy(Tc[:, c0:c1, :], bank(idx[f"t{l}"], g)).then_inc(outd, 1)
                    for st, dst in ((f"x{l}", Xc), (f"y{l}", Yc)):
                        if st in idx:
                            for g, (c0, c1) in enumerate(G3):
                                wait_full(dve, i, st, g)
                                dve.tensor_tensor(dst[:, c0:c1, :], dst[:, c0:c1, :], bank(idx[st], g),
                                                  ALU.subtract).then_inc(outd, 1)
                for g, (c0, c1) in enumerate(G3):
                    wait_full(dve, i, "H", g)
                    for lo, hi in halves:
                        ins = dve.tensor_copy(Hb[lo:hi, c0:c1, lo:hi], bank(idx["H"], g, lo, hi))
                    ins.then_inc(outd, 1)
                for g, (c0, c1) in enumerate(G3):
                    wait_full(dve, i, "E", g)
                    for lo, hi in halves:
                        ins = dve.tensor_tensor(Eb[lo:hi, c0:c1, lo:hi], bc(two[lo:hi], c1 - c0),
                                                bank(idx["E"], g, lo, hi), ALU.subtract)
                    ins.then_inc(outd, 1)
                for g, (c0, c1) in enumerate(G3):
                    c1 = min(c1, PC)
                    wait_full(dve, i, "N", g)
                    dve.tensor_tensor(Nc[:, c0:c1, :], bank(idx["N"], g, 0, P, 0, c1 - c0),
                                      pend[:, c0:c1].unsqueeze(2).broadcast_to([P, c1 - c0, HD]), ALU.mult).then_inc(outd, 1)
                wait_taken(dve, i, "N", 2)
                dve.tensor_copy(Sc[:, 0, :], Nc[:, 0, :]).then_inc(std, 1)
                for c in range(1, PC):
                    dve.wait_ge(stp, i * 16 + c)
                    dst = Sc[:, c, :] if c < PC - 1 else sout[:, 8, :]
                    dve.scalar_tensor_tensor(out=dst, in0=m.ps[:, 6 + c % 2, 0:HD], scalar=pend[:, c:c + 1],
                                             in1=Nc[:, c, :], op0=ALU.mult, op1=ALU.add).then_inc(std, 1)
                for g, (c0, c1) in enumerate(G3):
                    wait_full(dve, i, "W", g)
                    dve.tensor_tensor(Wc[:, c0:c1, :], BVc[:, c0:c1, :], bank(idx["W"], g), ALU.add).then_inc(outd, 1)
                for g, (t0, n) in enumerate(TB):
                    wait_full(dve, i, "mean", g)
                    dve.tensor_tensor(YC[:, t0:t0 + n], YT[:, t0:t0 + n], m.ps[:, 3 * (idx["mean"] % 2) + g, 0:n],
                                      ALU.subtract).then_inc(outd, 1)
                dve.wait_ge(stp, i * 16 + 16)
                dve.tensor_tensor(sout[:, 0:NB, :], m.ps[:, 6, :].rearrange("p (b v) -> p b v", b=NB), sbc, ALU.add)
                dve.drain()
                dve.tensor_tensor(sout[:, 0:NB, :], sout[:, 0:NB, :],
                                  pend[:, PC:PC + NB].unsqueeze(2).broadcast_to([P, NB, HD]), ALU.mult).then_inc(std, 1)
                wait_taken(dve, i, "var", 2)
                dve.reciprocal(SQ2, RS2)
                dve.drain()
                dve.scalar_tensor_tensor(out=YC, in0=YC, scalar=col(PLG), in1=SQ2, op0=ALU.mult, op1=ALU.mult)
                for g, (t0, n) in enumerate(TB):
                    wait_full(dve, i, "bonus", g)
                    dve.tensor_tensor(BB[:, t0:t0 + n], V[:, t0:t0 + n], m.ps[:, 3 * (idx["bonus"] % 2) + g, 0:n],
                                      ALU.mult).then_inc(outd, 1)
                wait_taken(dve, i, "bonus", 2)
                dve.wait_ge(out_s, i * 16 + 16)
                dve.scalar_tensor_tensor(out=YC, in0=YC, scalar=col(PLB), in1=BB, op0=ALU.add, op1=ALU.add)
                dve.drain()
                dve.tensor_tensor(m.H[:, bass.ds(i, 1), :].rearrange("p a t -> p (a t)"), YC, G, ALU.mult).then_inc(done, 1)

        @block.tensor
        def _(pe):
            pe.wait_ge(zeroed, 1)
            pe.wait_ge(consts, 7 * 16)
            with pe.Fori(0, PAIRS) as i:

                def free(st, g):
                    if idx[st] >= 2:
                        wait_taken(pe, i, ORDER[idx[st] - 2], g)

                def blocks(st, parts):
                    for g, (t0, n) in enumerate(TB):
                        free(st, g)
                        for q, (lhs, rhs) in enumerate(parts):
                            mm = pe.matmul(m.ps[:, 3 * (idx[st] % 2) + g, 0:n], lhs, rhs[:, t0:t0 + n],
                                           start=(q == 0), stop=(q == len(parts) - 1))
                        mm.then_inc(full, 1)

                def chunks(st, parts, before=None, last=NCH):
                    for g, (c0, c1) in enumerate(G3):
                        free(st, g)
                        if before is not None:
                            before(g)
                        for c in range(c0, min(c1, last)):
                            for q, (lhs, rhs) in enumerate(parts):
                                mm = pe.matmul(m.ps[:, 3 * (idx[st] % 2) + g, (c - c0) * C:(c - c0 + 1) * C], lhs[:, c, :],
                                               rhs[:, c, :] if len(rhs.shape) == 3 else rhs,
                                               start=(q == 0), stop=(q == len(parts) - 1))
                        mm.then_inc(full, 1)

                pe.wait_ge(loaded, i * 112 + 112)
                blocks("sig", [(lw2[0:64, 0, :], lora[0:64, 0, :])])
                blocks("a", [(lw2[64:128, 1, :], lora[64:128, 0, :])])
                blocks("g", [(lw2[:, 2, :], lora[:, 1, :]), (lw2[0:32, 3, :], lora[0:32, 2, :])])
                pe.wait_ge(prep_a, i * 7 + 1)
                blocks("kn", [(bones, EP)])
                pe.wait_ge(bdin, i * 1 + 1)
                chunks("at", [(Bb, Qch)])
                chunks("kq", [(Kb, Qch)])
                chunks("rb", [(Bb, Rch)])
                chunks("rk", [(Kb, Rch)])
                chunks("bt", [(Bb, two)])
                chunks("kt", [(Kb, two)])
                pe.wait_ge(copies, i * 1 + 1)
                chunks("vt", [(Vb, two)])
                chunks("qt", [(Qb, two)])
                chunks("bv", [(KQb, Vc)], lambda g: wait_taken(pe, i, "vt", g))
                chunks("t0", [(AMb, two)], lambda g: pe.wait_ge(am, i * 18 + g + 1))
                for l in range(1, 6):
                    def ready_t(g):
                        pe.wait_ge(am, i * 18 + 3 * l + g + 1)
                        wait_taken(pe, i, f"x{l - 1}" if l > 1 else "t0", g)
                    chunks(f"t{l}", [(AMb, Xc)], ready_t)
                    def ready_x(g):
                        pe.wait_ge(yb, i * 18 + 3 * (l - 1) + g + 1)
                        wait_taken(pe, i, f"t{l}", g)
                    if l < 5:
                        chunks(f"x{l}", [(Yb, Tc)], ready_x)
                    chunks(f"y{l}", [(TBb, Yc)], lambda g: pe.wait_ge(tb, i * 15 + 3 * (l - 1) + g + 1))
                chunks("G", [(Yb, BVc)], lambda g: pe.wait_ge(yb, i * 18 + 15 + g + 1))
                chunks("H", [(Yb, Qtc)])
                chunks("E", [(Hb, Btc)], lambda g: wait_taken(pe, i, "H", g))
                chunks("N", [(BTb, Gc), (KTb, Vc)], lambda g: wait_taken(pe, i, "G", g))
                wait_taken(pe, i, "E", 2)
                for c in range(1, PC):
                    pe.wait_ge(std, i * 17 + c)
                    pe.matmul(m.ps[:, 6 + c % 2, 0:HD], Eb[:, c, :], Sc[:, c - 1, :], start=True, stop=True).then_inc(stp, 1)
                pe.wait_ge(std, i * 17 + PC)
                for g, (c0, c1) in enumerate(G3):
                    free("W", g)
                    for c in range(c0, c1):
                        dst = m.ps[:, 3 * (idx["W"] % 2) + g, (c - c0) * C:(c - c0 + 1) * C]
                        if c == 0:
                            mm = pe.matmul(dst, Qb[:, 0, :], zeros, start=True, stop=True)
                        elif c < PC:
                            mm = pe.matmul(dst, Qb[:, c, :], Sc[:, c - 1, :], start=True, stop=True)
                        else:
                            for b in range(NB):
                                mm = pe.matmul(dst, qm[:, b * P:(b + 1) * P], sbc[:, b, :], start=(b == 0), stop=(b == NB - 1))
                    mm.then_inc(full, 1)
                chunks("U", [(Yb, Wc)], lambda g: wait_taken(pe, i, "W", g))
                for g, (c0, c1) in enumerate(G3):
                    free("Y", g)
                    pe.wait_ge(ub, i * 3 + g + 1)
                    pe.wait_ge(sb2, i * 3 + g + 1)
                    for c in range(c0, c1):
                        dst = m.ps[:, 3 * (idx["Y"] % 2) + g, (c - c0) * C:(c - c0 + 1) * C]
                        sampled = c == SC
                        if sampled:
                            for b in range(NB):
                                pe.matmul(dst[:, b * NS:(b + 1) * NS], sbb[:, b, :], Rch[:, c, b * NS:(b + 1) * NS],
                                          start=(b == 0), stop=False, skip_group_check=True)
                        elif c:
                            pe.matmul(dst, Sb[:, c, :], Rch[:, c, :], start=True, stop=False)
                        pe.matmul(dst, Ub[:, c, :], RBc[:, c, :], start=(c == 0), stop=False, skip_group_check=sampled)
                        mm = pe.matmul(dst, VTb[:, c, :], RKc[:, c, :], start=False, stop=True, skip_group_check=sampled)
                    mm.then_inc(full, 1)
                for g, (t0, n) in enumerate(TB):
                    free("mean", g)
                    wait_taken(pe, i, "Y", g)
                    pe.matmul(m.ps[:, 3 * (idx["mean"] % 2) + g, 0:n], mean64, YT[:, t0:t0 + n], start=True, stop=True).then_inc(full, 1)
                pe.wait_ge(masked, i * 1 + 1)
                pe.matmul(m.ps[:, 6, :], BTb[:, SC, :], um.rearrange("p b v -> p (b v)"), start=True, stop=False)
                pe.matmul(m.ps[:, 6, :], KTb[:, SC, :], vm.rearrange("p b v -> p (b v)"), start=False, stop=True).then_inc(stp, 1)
                pe.wait_ge(prep_a, i * 7 + 7)
                blocks("var", [(mean64, SQ2)])
                blocks("bonus", [(bones, RKR)])


AO_TILE = 13


def prompt_attention(m, a, scratch):
    nc = m.nc
    with ExitStack() as ctx:
        sem = lambda n: ctx.enter_context(nc.semaphore(f"pa_{n}"))
        consts, zeroed, proj, pta, ptd, roped, vfull, vtaken, kvst = (
            sem(n) for n in ("consts", "zeroed", "proj", "proj_act", "proj_dve", "roped", "v_psum", "v_tok", "kv_stored"))
        sfull, biased, maxed, expd, ptfull, pt, nfull, ntaken = (
            sem(n) for n in ("scores", "biased", "maxed", "exp", "pt_psum", "pt", "out_psum", "out"))
        diff, wexp, merged = sem("diff"), sem("weight_exp"), sem("merged")
        wl = [sem(f"wl{n}") for n in range(9)]
        bt = lambda n, c=1: m.big[:, n * T:(n + c) * T]
        Q, K, V, R = bt(0), bt(1), bt(2), bt(3)
        NMZ = [tiles(m.big, (4 + 3 * g) * T, 3, T) for g in range(3)]
        AO = tiles(m.big, AO_TILE * T, AP_, T)
        Vt = m.big[:, 17 * T:17 * T + 8 * P].rearrange("p (n j) -> p n j", n=8)
        COS, SIN = bt(18), bt(19)
        SM = [m.big[:, (20 * T + s * 1024):(20 * T + s * 1024 + 512)].rearrange("p (h k) -> p h k", h=2) for s in range(2)]
        PT = [m.big[:, (20 * T + s * 1024 + 512):(20 * T + s * 1024 + 1024)].rearrange("p (h k q) -> p h k q", h=2, k=2)
              for s in range(2)]
        slots = [tiles(m.w, n * D, KT, P) for n in range(5)] + [tiles(m.tmp, n * D, KT, P) for n in range(4)]
        o = 4 * D
        masks = m.tmp[:, o:o + 3 * P].rearrange("p (n k) -> p n k", n=3)
        rot = m.tmp[:, o + 384:o + 512]
        nm = m.tmp[:, o + 512:o + 528].rearrange("p (i h) -> p i h", i=8)
        zz = m.tmp[:, o + 528:o + 544].rearrange("p (i h) -> p i h", i=8)

        def tok(ap, g, i):
            if g == 0:
                return ap[..., i * P:(i + 1) * P]
            if g == 1:
                lead = "p" if len(ap.shape) == 2 else "p c"
                return ap[..., 0:SEQ].rearrange(f"{lead} (n j r) -> {lead} n r j", n=2, r=4)[..., i // 4, i % 4, :]
            lead = "p" if len(ap.shape) == 2 else "p c"
            return ap[..., 0:SEQ].rearrange(f"{lead} (j r) -> {lead} r j", r=16)[..., 2 * i:2 * i + 2, :]

        def stationary(ap, g, i):
            if g < 2:
                return [(slice(0, P), tok(ap, g, i))]
            one = ap[:, 0:SEQ].rearrange("p (j r) -> p r j", r=16)
            return [(slice(64 * r, 64 * r + 64), one[:, 2 * i + r, :]) for r in range(2)]

        def before(g, i):
            return (i - 1 if g == 0 and i else i - 4 if g == 1 and i >= 4 else None)

        block = ctx.enter_context(nc.Block())

        @block.sync
        def _(sp):
            for t, n in ((masks, "c_amask"), (rot, "c_rot"), (COS, "c_cos"), (SIN, "c_sin")):
                sp.dma_start(t, a[n]).then_inc(consts, 16)
            with sp.Fori(0, AP_) as i:
                for g in range(3):
                    for s in range(3):
                        sp.wait_ge(proj, i * 45 + (15 * g + (3, 6, 15)[s]))
                        sp.dma_start(slots[3 * g + s], a["wqkv"][bass.ds(i + (s * 12 + g * 4), 1)].rearrange(
                            "a p k c -> p (a k) c")).then_inc(wl[3 * g + s], 16)
                for g in range(3):
                    sp.wait_ge(roped, i * 6 + 2 * g + 2)
                    for n, t in ((0, Q), (1, K)):
                        sp.dma_start(scratch[n, bass.ds(i + g * 4, 1)].rearrange("a p t -> p (a t)"), t[:, SEQ:T]).then_inc(kvst, 16)
                    sp.dma_start(a["o_k"][bass.ds(i + g * 4, 1)].rearrange("a p t -> p (a t)"), K).then_inc(kvst, 16)
                    sp.wait_ge(pta, i * 27 + 9 * g + 9)
                    sp.dma_start(scratch[2, bass.ds(i + g * 4, 1)].rearrange("a p t -> p (a t)"), V[:, SEQ:T]).then_inc(kvst, 16)
                    sp.dma_start(a["o_v"][bass.ds(i + g * 4, 1)].rearrange("a p t -> p (a t)"), V).then_inc(kvst, 16)
            sp.wait_ge(kvst, 16 * 5 * 3 * AP_)

        @block.tensor
        def _(pe):
            pe.sem_inc(proj, 45)
            pe.wait_ge(consts, 64)
            with pe.Fori(0, AP_) as i:
                for g in range(3):
                    def product(s, base, dest):
                        pe.wait_ge(wl[3 * g + s], i * 16 + 16)
                        for b, (t0, n) in enumerate(TB):
                            if s == 2:
                                pe.wait_ge(ptd, i * 18 + 6 * g + b + 1)
                            for k in range(KT):
                                mm = pe.matmul(m.ps[:, base + b, 0:n], slots[3 * g + s][:, k, :], m.H[:, k, t0:t0 + n],
                                               start=(k == 0), stop=(k == KT - 1))
                            mm.then_inc(proj, 1)

                    def rotate(n_, src, base):
                        for b, (t0, n) in enumerate(TB):
                            pe.wait_ge(pta, i * 27 + 9 * g + 3 * n_ + b + 1)
                            pe.matmul(m.ps[:, base + b, 0:n], rot, src[:, t0:t0 + n], start=True, stop=True).then_inc(proj, 1)

                    if g:
                        pe.wait_ge(pt, i * 24 + 8 * g)
                    else:
                        pe.wait_ge(merged, i * 1 + 1)
                    product(0, 0, Q)
                    product(1, 3, K)
                    rotate(0, Q, 0)
                    rotate(1, K, 3)
                    product(2, 0, V)
                    if g:
                        pe.wait_ge(ntaken, i * 24 + 8 * g)
                    pe.wait_ge(pta, i * 27 + 9 * g + 9)
                    for i8 in range(8):
                        for rows, lhs in stationary(V, g, i8):
                            dst = m.ps[rows, 6 + i8 // 4, (i8 % 4) * P:(i8 % 4 + 1) * P]
                            if g < 2:
                                mm = pe.transpose(dst, lhs, m.ident[:, :])
                            else:
                                mm = pe.matmul(dst, lhs, m.ident[:, :], start=True, stop=True)
                        if i8 % 4 == 3:
                            mm.then_inc(vfull, 1)
                    pe.wait_ge(roped, i * 6 + 2 * g + 2)
                    pe.wait_ge(vtaken, i * 6 + 2 * g + 2)

                    def scores(n):
                        if n >= 2:
                            pe.wait_ge(biased, i * 24 + 8 * g + n - 1)
                        for h in range(2):
                            r = slice(64 * h, 64 * h + 64)
                            for q, kt in ((0, before(g, n)), (1, n)):
                                if kt is None:
                                    continue
                                lhs = tok(Q[r], g, n) if g < 2 else R[r, n * P:(n + 1) * P]
                                mm = pe.matmul(m.ps[:, 2 * (n % 2) + h, q * P:(q + 1) * P], lhs, tok(K[r], g, kt),
                                               start=True, stop=True)
                        mm.then_inc(sfull, 1)

                    def turn(n):
                        pe.wait_ge(expd, i * 24 + 8 * g + n + 1)
                        if n >= 2:
                            pe.wait_ge(pt, i * 24 + 8 * g + n - 1)
                        for h in range(2):
                            for q in range(2):
                                if q or before(g, n) is not None:
                                    mm = pe.transpose(m.ps[:, 4 + n % 2, (2 * h + q) * P:(2 * h + q + 1) * P],
                                                      SM[n % 2][:, h, q * P:(q + 1) * P], m.ident[:, :])
                        mm.then_inc(ptfull, 1)

                    def values(n):
                        pe.wait_ge(pt, i * 24 + 8 * g + n + 1)
                        if n >= 2:
                            pe.wait_ge(ntaken, i * 24 + 8 * g + n - 1)
                        ps = m.ps[:, 6 + n % 2, :]
                        b4 = before(g, n)
                        for h in range(2):
                            if b4 is not None:
                                pe.matmul(ps[64 * h:64 * h + 64, 0:P], Vt[:, b4, 64 * h:64 * h + 64], PT[n % 2][:, h, 0, :],
                                          start=True, stop=False)
                            pe.matmul(ps[64 * h:64 * h + 64, 0:P], Vt[:, n, 64 * h:64 * h + 64], PT[n % 2][:, h, 1, :],
                                      start=(b4 is None), stop=True)
                        for q, t in ((1, nm), (2, zz)):
                            for h in range(2):
                                mm = pe.matmul(ps[64 * h:64 * h + 64, q * P:(q + 1) * P],
                                               t[:, n, h:h + 1].broadcast_to([P, 64]), m.ident[:, :], start=True, stop=True)
                        mm.then_inc(nfull, 1)

                    for n in range(10):
                        if n < 8:
                            scores(n)
                        if 1 <= n <= 8:
                            turn(n - 1)
                        if n >= 2:
                            values(n - 2)

        @block.scalar
        def _(act):
            with act.Fori(0, AP_) as i:
                for g in range(3):
                    for s, (dst, base, at) in enumerate(((Q, 0, 3), (K, 3, 6), (V, 0, 15))):
                        for b, (t0, n) in enumerate(TB):
                            act.wait_ge(proj, i * 45 + (45 + 15 * g + at - 3 + b + 1))
                            act.activation(dst[:, t0:t0 + n], m.ps[:, base + b, 0:n], ACT.Copy).then_inc(pta, 1)
                    for q in range(2):
                        act.wait_ge(vfull, i * 6 + 2 * g + q + 1)
                        act.activation(Vt[:, 4 * q:4 * q + 4, :].rearrange("p n j -> p (n j)"), m.ps[:, 6 + q, :],
                                       ACT.Copy).then_inc(vtaken, 1)

                    def exps(n):
                        act.wait_ge(maxed, i * 24 + 8 * g + n + 1)
                        lo = 0 if before(g, n) is not None else P
                        for h in range(2):
                            ins = act.activation(SM[n % 2][:, h, lo:2 * P], SM[n % 2][:, h, lo:2 * P], ACT.Exp,
                                                 bias=nm[:, n, h:h + 1], accum_out=zz[:, n, h:h + 1])
                        ins.then_inc(expd, 1)

                    def take(n):
                        act.wait_ge(ptfull, i * 24 + 8 * g + n + 1)
                        if n >= 2:
                            act.wait_ge(nfull, i * 24 + 8 * g + n - 1)
                        ps = m.ps[:, 4 + n % 2, :].rearrange("p (h k q) -> p h k q", h=2, k=2)
                        lo = 0 if before(g, n) is not None else 1
                        act.activation(PT[n % 2][:, :, lo:2, :], ps[:, :, lo:2, :], ACT.Copy).then_inc(pt, 1)

                    for n in range(9):
                        if n < 8:
                            exps(n)
                        if n >= 1:
                            take(n - 1)
                    act.wait_ge(kvst, i * 240 + (80 * g + 80))
                for g in range(3):
                    act.wait_ge(diff, i * 3 + g + 1)
                    act.activation(NMZ[g][:, 1, 0:SEQ], NMZ[g][:, 1, 0:SEQ], ACT.Exp).then_inc(wexp, 1)

        @block.vector
        def _(dve):
            dve.wait_ge(consts, 64)
            dve.nop().then_inc(merged, 1)
            with dve.Fori(0, AP_) as i:
                for g in range(3):
                    for n_, (t, base) in enumerate(((Q, 0), (K, 3))):
                        for b, (t0, n) in enumerate(TB):
                            dve.wait_ge(proj, i * 45 + (45 + 15 * g + 6 + 3 * n_ + b + 1))
                            dve.tensor_tensor(R[:, t0:t0 + n], m.ps[:, base + b, 0:n], SIN[:, t0:t0 + n], ALU.mult).then_inc(ptd, 1)
                        dve.tensor_tensor(t, t, COS, ALU.mult)
                        dve.drain()
                        last = dve.tensor_tensor(t, t, R, ALU.add)
                        if g == 2 and n_ == 1:
                            dve.drain()
                            last = dve.tensor_copy(R[:, 0:SEQ].rearrange("p (r j) -> p r j", r=16),
                                                   Q[:, 0:SEQ].rearrange("p (j r) -> p r j", r=16))
                        last.then_inc(roped, 1)
                        dve.drain()
                    for n in range(10):
                        if n < 8:
                            b4 = before(g, n)
                            lo, k0 = (0, 0) if b4 is not None else (P, 1)
                            dve.wait_ge(sfull, i * 24 + 8 * g + n + 1)
                            if n >= 2:
                                dve.wait_ge(ptfull, i * 24 + 8 * g + n - 1)
                            src = m.ps[:, 2 * (n % 2):2 * (n % 2) + 2, lo:2 * P]
                            mk = masks[:, k0:2, :].rearrange("p n k -> p (n k)") if g < 2 else masks[:, 2, :]
                            dve.scalar_tensor_tensor(out=SM[n % 2][:, :, lo:2 * P], in0=src, scalar=SCALE,
                                                     in1=mk.unsqueeze(1).broadcast_to([P, 2, 2 * P - lo]),
                                                     op0=ALU.mult, op1=ALU.add).then_inc(biased, 1)
                            dve.wait_ge(biased, i * 24 + 8 * g + n + 1)
                            dve.tensor_reduce(nm[:, n, :], SM[n % 2][:, :, lo:2 * P], AX.X, ALU.max,
                                              negate=True).then_inc(maxed, 1)
                        if n >= 2:
                            dve.wait_ge(nfull, i * 24 + 8 * g + n - 1)
                            src = m.ps[:, 6 + n % 2, 0:3 * P].rearrange("p (c q) -> p c q", c=3)
                            dst = tok(NMZ[g], g, n - 2)
                            if g == 2:
                                src = src.rearrange("p c (r j) -> p c r j", r=2)
                            dve.tensor_copy(dst, src).then_inc(ntaken, 1)
                N, M, Z = ([NMZ[g][:, c, 0:SEQ] for g in range(3)] for c in range(3))
                low = R[:, 0:SEQ]
                dve.drain()
                dve.tensor_tensor(low, M[0], M[1], ALU.min)
                dve.drain()
                dve.tensor_tensor(low, low, M[2], ALU.min)
                dve.drain()
                for g in range(3):
                    dve.tensor_tensor(M[g], low, M[g], ALU.subtract).then_inc(diff, 1)
                for g in range(3):
                    dve.wait_ge(wexp, i * 3 + g + 1)
                    dve.tensor_tensor(N[g], N[g], M[g], ALU.mult)
                    dve.tensor_tensor(Z[g], Z[g], M[g], ALU.mult)
                dve.drain()
                dve.tensor_tensor(N[0], N[0], N[1], ALU.add)
                dve.tensor_tensor(Z[0], Z[0], Z[1], ALU.add)
                dve.drain()
                dve.tensor_tensor(N[0], N[0], N[2], ALU.add)
                dve.tensor_tensor(Z[0], Z[0], Z[2], ALU.add)
                dve.drain()
                dve.reciprocal(Z[1], Z[0])
                dve.drain()
                dve.tensor_tensor(AO[:, bass.ds(i, 1), 0:SEQ].rearrange("p a t -> p (a t)"), N[0], Z[1],
                                  ALU.mult).then_inc(merged, 1)


def sampled_attention(m, a, scratch):
    nc = m.nc
    NK, CW = 9, (320, 512, 512)
    ROUNDS = NB // 2
    with ExitStack() as ctx:
        sem = lambda n: ctx.enter_context(nc.semaphore(f"sa_{n}"))
        qkv_in, zeroed, vtfull, vtaken, mk, qrow, sfull, biased, maxed, expd, normed, ptfull, pt, ofull, otaken = (
            sem(n) for n in ("qkv_in", "zeroed", "v_psum", "v_tok", "mask", "q_rows", "scores", "biased", "maxed",
                             "exp", "normed", "pt_psum", "pt", "out_psum", "out"))
        kin = [sem(f"k{b}") for b in range(2)]
        vin = [sem(f"v{b}") for b in range(2)]
        AO = tiles(m.big, AO_TILE * T, AP_, T)
        w9 = NK * 512
        kt = [m.big[:, b * w9:(b + 1) * w9].rearrange("p (n k) -> p n k", n=4) for b in range(2)]
        vv = [m.big[:, o:o + w9].rearrange("p (n c) -> p n c", n=NK) for o in (2 * w9, 17 * T)]
        small = lambda o, w: m.h[:, o:o + w]
        q12, k12, v12 = (small(768 * n, 768).rearrange("p (g c t) -> p g c t", g=3, c=AP_) for n in range(3))
        vs = small(2304, 1536).rearrange("p (g c) -> p g c", g=3)
        qr = small(3840, 1536).rearrange("p (b g c r) -> p b g c r", b=2, g=3, c=AP_)
        nm, zz, rz = (small(5376 + n, 1) for n in range(3))
        ss = m.w[:, 0:sum(CW)]
        ptb = m.w[:, 1344:1344 + 12 * P].rearrange("p (n r) -> p n r", n=12)
        mask = m.tmp[:, 0:sum(CW)]
        block = ctx.enter_context(nc.Block())

        @block.sync
        def _(sp):
            for n, t in enumerate((q12, k12, v12)):
                sp.dma_start(t.rearrange("p g c t -> p (g c) t"), scratch[n].rearrange("n p t -> p n t")).then_inc(qkv_in, 16)
            with sp.Fori(0, ROUNDS) as i:
                for b in range(2):
                    sp.wait_ge(sfull, i * 1 + 1)
                    sp.dma_start(kt[b], a["kT"][bass.ds(i * 2 + b, 1)].rearrange("a p n k -> p (a n) k")).then_inc(kin[b], 16)
                sp.wait_ge(biased, i * 3 + 3)
                sp.dma_start(mask, a["c_smask"][bass.ds(i, 1)].rearrange("a p k -> p (a k)")).then_inc(mk, 16)
                for b in range(2):
                    sp.wait_ge(ofull, i * 1 + 1)
                    sp.dma_start(vv[b], a["vc"][bass.ds(i * 2 + b, 1)].rearrange("a p n k -> p (a n) k")).then_inc(vin[b], 16)

        @block.gpsimd
        def _(pool):
            pool.memset(small(3840, 1536), 0.0).then_inc(zeroed, 1)

        @block.tensor
        def _(pe):
            pe.sem_inc(sfull, 1)
            pe.sem_inc(ofull, 1)
            pe.wait_ge(qkv_in, 48)
            for g in range(3):
                for c in range(AP_):
                    mm = pe.transpose(m.ps[0:64, g, c * P:(c + 1) * P], v12[:, g, c, :], m.ident[:, :])
                mm.then_inc(vtfull, 1)
            pe.wait_ge(vtaken, 3)
            with pe.Fori(0, ROUNDS) as i:
                pe.wait_ge(qrow, i * 1 + 1)
                for b in range(2):
                    pe.wait_ge(kin[b], i * 16 + 16)
                    rows = slice(64 * b, 64 * b + 64)
                    if b == 0:
                        pe.wait_ge(biased, i * 3 + 3)
                    jobs = [(0, 0, P, 0, lambda c: kt[b][:, c, 0:P])]
                    for g in range(3):
                        jobs.append((0, P + 64 * g, 64, g, lambda c, g=g: k12[:, g, c, :]))
                    jobs.append((1, 0, 512, 1, lambda c: kt[b][:, c, P:P + 512]))
                    jobs.append((2, 0, 512, 2, lambda c: kt[b][:, c, P + 512:P + 1024]))
                    for bank, c0, n, g, rhs in jobs:
                        for c in range(AP_):
                            mm = pe.matmul(m.ps[rows, bank, c0:c0 + n], qr[:, b, g, c, :], rhs(c), start=(c == 0), stop=(c == AP_ - 1))
                mm.then_inc(sfull, 1)
                pe.wait_ge(normed, i * 1 + 1)
                cols = [(0, P)] + [(320 + P * n, P) for n in range(8)] + [(P + 64 * n, 64) for n in range(3)]
                for n, (c0, w) in enumerate(cols):
                    mm = pe.transpose(m.ps[0:w, 3 + n // 4, (n % 4) * P:(n % 4 + 1) * P] if n < 8 else
                                      m.ps[0:w, 5, (n - 8) * P:(n - 7) * P], ss[:, c0:c0 + w], m.ident[:, :])
                    if n in (3, 7, 11):
                        mm.then_inc(ptfull, 1)
                for b in range(2):
                    pe.wait_ge(vin[b], i * 16 + 16)
                    for c in range(AP_):
                        for n in range(12):
                            if n < NK:
                                lhs, rhs = vv[b][:, n, c * P:(c + 1) * P], ptb[:, n, 64 * b + 16 * c:64 * b + 16 * c + 16]
                            else:
                                lhs, rhs = vs[0:64, n - NK, c * P:(c + 1) * P], ptb[0:64, n, 64 * b + 16 * c:64 * b + 16 * c + 16]
                            if b == 0 and c == 0 and n in (0, 4, 8):
                                pe.wait_ge(pt, i * 4 + (n // 4 + 1 if n < 8 else 4))
                            mm = pe.matmul(m.ps[:, 7, (4 * b + c) * 16:(4 * b + c + 1) * 16], lhs, rhs, start=(n == 0), stop=(n == 11))
                mm.then_inc(ofull, 1)

        @block.scalar
        def _(act):
            for g in range(3):
                act.wait_ge(vtfull, g + 1)
                act.activation(vs[0:64, g, :], m.ps[0:64, g, :], ACT.Copy).then_inc(vtaken, 1)
            with act.Fori(0, ROUNDS) as i:
                act.wait_ge(maxed, i * 1 + 1)
                act.activation(ss, ss, ACT.Exp, bias=nm, accum_out=zz).then_inc(expd, 1)
                for n, (lo, hi, bank) in enumerate(((0, 4, 3), (4, 8, 4))):
                    act.wait_ge(ptfull, i * 3 + n + 1)
                    act.activation(ptb[:, lo:hi, :].rearrange("p n r -> p (n r)"), m.ps[:, bank, :], ACT.Copy).then_inc(pt, 1)
                act.wait_ge(ptfull, i * 3 + 3)
                act.activation(ptb[:, 8, :], m.ps[:, 5, 0:P], ACT.Copy).then_inc(pt, 1)
                act.activation(ptb[0:64, 9:12, :].rearrange("p n r -> p (n r)"), m.ps[0:64, 5, P:4 * P], ACT.Copy).then_inc(pt, 1)

        @block.vector
        def _(dve):
            dve.wait_ge(zeroed, 1)
            dve.wait_ge(qkv_in, 48)
            for _n in range(3):
                dve.nop().then_inc(biased, 1)
            with dve.Fori(0, ROUNDS) as i:
                dve.wait_ge(sfull, i * 1 + 1)
                for c in range(AP_):
                    for h in range(2):
                        for g in range(3):
                            src = q12[64 * h:64 * h + 64, g, c, bass.ds(i * 16, 16)].rearrange("p (b t) -> p b t", b=2)
                            r0 = (2 * c + h) * NS
                            ins = dve.tensor_copy(qr[64 * h:64 * h + 64, :, g, c, r0:r0 + NS], src)
                ins.then_inc(qrow, 1)
                dve.wait_ge(mk, i * 16 + 16)
                dve.wait_ge(sfull, i * 1 + 2)
                c0 = 0
                for n in range(3):
                    dve.scalar_tensor_tensor(out=ss[:, c0:c0 + CW[n]], in0=m.ps[:, n, 0:CW[n]], scalar=SCALE,
                                             in1=mask[:, c0:c0 + CW[n]], op0=ALU.mult, op1=ALU.add).then_inc(biased, 1)
                    c0 += CW[n]
                dve.wait_ge(biased, i * 3 + 6)
                dve.tensor_reduce(nm, ss, AX.X, ALU.max, negate=True).then_inc(maxed, 1)
                dve.wait_ge(expd, i * 1 + 1)
                dve.reciprocal(rz, zz)
                dve.drain()
                dve.tensor_scalar(ss, ss, rz, None, ALU.mult).then_inc(normed, 1)
                dve.wait_ge(ofull, i * 1 + 2)
                for h in range(2):
                    src = m.ps[64 * h:64 * h + 64, 7, 0:P].rearrange("p (b c g t) -> p b c g t", b=2, c=AP_, g=2)[:, :, :, h, :]
                    for b in range(2):
                        dve.tensor_copy(AO[64 * h:64 * h + 64, :, bass.ds(i * 16 + (SEQ + 8 * b), NS)], src[:, b])


def hybrid_step(nc, a):
    rkv = nc.dram_tensor("rkv_scratch", [3 * PAIRS, P, T], F32, kind="Internal").ap()
    qkv = nc.dram_tensor("qkv_scratch", [3, 3 * AP_, P, NB * NS], F32, kind="Internal").ap()
    with ExitStack() as ctx:
        m = Machine(nc, ctx)
        load_constants(m, a)
        rmsnorm(m, 0, m.X)
        rwkv_inputs(m, a, rkv)
        rwkv_core(m, a, rkv)
        mixed = tiles(m.big, 0, KT, T)
        dense(m, "rwo", a["wo"], KT, m.H, mixed)
        rmsnorm(m, 1, mixed, add=True, reload=a["xT"])
        rmsnorm(m, 2, m.X)
        ffn(m, a, 0)
        rmsnorm(m, 3, m.H, add=True)
        rmsnorm(m, 4, m.X)
        prompt_attention(m, a, qkv)
        sampled_attention(m, a, qkv)
        dense(m, "awo", a["at_wo"], AP_, tiles(m.big, AO_TILE * T, AP_, T), m.H)
        rmsnorm(m, 5, m.H, add=True)
        rmsnorm(m, 6, m.X)
        ffn(m, a, 1)
        rmsnorm(m, 7, m.H, add=True)
        store_y(m, a)


def _tiled(w):
    k, n = w.shape
    return np.ascontiguousarray(w.reshape(k // P, P, n // P, P).transpose(2, 1, 0, 3))


def _channels(x):
    t, c = x.shape
    return np.ascontiguousarray(x.T.reshape(c // P, P, t).transpose(1, 0, 2))


def _constants():
    f = np.float32
    i = np.arange(P)
    head, tok = i // C, i % C
    c = {}
    c["c_ident"] = np.eye(P, dtype=f)
    c["c_ones"] = np.ones((P, P), f)
    c["c_bones"] = (head[:, None] == head[None, :]).astype(f)
    c["c_mean64"] = c["c_bones"] / f(HD)
    c["c_two"] = (tok[:, None] == np.arange(C)[None, :]).astype(f)
    lm = np.zeros((P, 6, P), f)
    for l in range(6):
        b = tok >> l
        lm[:, l, :] = (head[:, None] == head[None]) & (b[:, None] % 2 == 0) & (b[None] == b[:, None] + 1)
    c["c_level"] = lm
    s, t = tok[:, None], np.arange(C)[None]
    same = s // NS == t // NS
    c["c_masks"] = np.stack([s < t, s <= t, (s < t) & same, (s <= t) & same], 1).astype(f)
    c["c_rowb"] = (tok[:, None] // NS == np.arange(NB)[None]).astype(f)
    r = np.ones(T, f)
    r[0:SEQ:C] = 0
    r[SEQ:T:NS] = 0
    c["c_reset"] = np.tile(r, (P, 1))
    e = i % HD
    rot = np.zeros((P, P), f)
    for d in range(P):
        if e[d] < 8:
            rot[d + 8, d] = -1
        elif e[d] < 16:
            rot[d - 8, d] = 1
    c["c_rot"] = rot
    pos = np.concatenate([np.arange(SEQ), np.tile(SEQ + np.arange(NS), NB)]).astype(f)
    inv = np.power(f(500000.0), -np.arange(8, dtype=f) / f(8)).astype(f)
    ang = (pos[None, :] * inv[e % 8][:, None]).astype(f)
    turned = (e < 16)[:, None]
    c["c_cos"] = np.where(turned, np.cos(ang), 1).astype(f)
    c["c_sin"] = np.where(turned, np.sin(ang), 0).astype(f)
    q, kk = i[:, None], i[None]
    c["c_amask"] = np.stack([np.where(kk >= q, 0, NEG), np.where(kk <= q, 0, NEG),
                             np.where((kk <= q) & (kk // 64 == q // 64), 0, NEG)], 1).astype(f)
    rb, rt = i // 64, i % NS
    sm = np.full((NB // 2, P, 1344), NEG, f)
    for rnd in range(NB // 2):
        k0 = np.arange(128)
        sm[rnd][:, 0:128] = np.where(k0[None] >= rt[:, None], 0, NEG)
        nb_, nt = np.arange(64) // NS, np.arange(64) % NS
        for g, (_w, dil) in enumerate(GROUPS3):
            d = rt[:, None] - nt[None]
            ok = (nb_[None] == (2 * rnd + rb)[:, None]) & (d >= 0) & (d % dil == 0)
            sm[rnd][:, 128 + 64 * g:192 + 64 * g] = np.where(ok, 0, NEG)
        k1 = np.arange(512)
        ok = (k1[None] >= rt[:, None]) & ((k1[None] - rt[:, None]) % 4 == 0)
        sm[rnd][:, 320:832] = np.where(ok, 0, NEG)
        ok = (k1[None] % 8) == rt[:, None]
        sm[rnd][:, 832:1344] = np.where(ok, 0, NEG)
    c["c_smask"] = sm
    return c


def _by_channel(v):
    return np.ascontiguousarray(np.moveaxis(v.reshape(*v.shape[:-1], -1, P), -1, 0).reshape(P, -1))


def _rwkv_arrays(inp):
    r = {}
    g = lambda n: np.asarray(inp[n])[0]
    r["mu"] = _by_channel(g("rw_mu")).reshape(P, 6, KT)
    r["shiftT"] = _channels(g("state_shift"))
    lw1 = np.concatenate([g("rw_w1"), g("rw_a1"), g("rw_g1")], 1)
    r["lw1"] = np.ascontiguousarray(lw1.reshape(KT, P, -1).transpose(1, 0, 2))
    r["wrkv"] = np.concatenate([_tiled(g(n)) for n in ("rw_wr", "rw_wk", "rw_wv")])
    r["wo"] = _tiled(g("rw_wo"))
    lw2 = np.zeros((PAIRS, P, 4, P), np.float32)
    cut = lambda w: w.reshape(w.shape[0], PAIRS, P).transpose(1, 0, 2)
    lw2[:, 0:64, 0] = cut(g("rw_w2"))
    lw2[:, 64:128, 1] = cut(g("rw_a2"))
    lw2[:, :, 2] = cut(g("rw_g2")[0:P])
    lw2[:, 0:32, 3] = cut(g("rw_g2")[P:])
    r["lw2"] = lw2
    pv = np.zeros((PAIRS, P, 8), np.float32)
    for j, n in enumerate(("rw_w0", "rw_a0", "rw_kk", "rw_ka", "rw_rk", "rw_lnx_g", "rw_lnx_b")):
        pv[:, :, j] = g(n).reshape(PAIRS, P)
    r["pv"] = pv
    s0 = g("state_wkv").reshape(NB, PAIRS, 2, HD, HD).transpose(1, 2, 4, 0, 3)
    r["s0c"] = np.ascontiguousarray(s0).reshape(PAIRS, P, NB, HD)
    bd = np.zeros((PAIRS, 2, HD, NB, 2, HD), np.float32)
    for h in range(2):
        bd[:, h, :, :, h] = s0[:, h]
    r["s0bd"] = bd.reshape(PAIRS, P, NB, P)
    return r


def _attention_arrays(inp):
    r = {}
    r["wqkv"] = _tiled(np.asarray(inp["at_wqkv"])[0])
    r["at_wo"] = _tiled(np.asarray(inp["at_wo"])[0])
    c0 = np.asarray(inp["cache_kv_w128"])[0]
    c1 = np.asarray(inp["cache_kv_w512"])[0]
    c2 = np.asarray(inp["cache_kv_w2048"])[0]
    c2 = c2.reshape(NB, SEQ // 16, 16, 2, 8, HD)[:, :, 0:NS].reshape(NB, -1, 2, 8, HD)
    kv = np.concatenate([c0, c1, c2], 1)
    nk = kv.shape[1]
    r["kT"] = np.ascontiguousarray(kv[:, :, 0].reshape(NB, nk, AP_, P).transpose(0, 3, 2, 1))
    r["vc"] = np.ascontiguousarray(kv[:, :, 1].reshape(NB, nk // P, P, AP_ * P).transpose(0, 2, 1, 3))
    return r


def _ffn_arrays(inp):
    r = {}
    r["wup"] = np.stack([_tiled(w) for w in np.asarray(inp["ff_wup"])])
    r["wdown"] = np.stack([_tiled(w) for w in np.asarray(inp["ff_wdown"])])
    cw, cb, st = (np.asarray(inp[n]) for n in ("ff_conv_w", "ff_conv_b", "state_conv"))
    vec = np.zeros((2, FT, P, 40), np.float32)
    cc = np.concatenate([cw, cb[:, None]], 1).reshape(2, 4, 2, FT, P)
    vec[..., 0:8] = cc.transpose(0, 3, 4, 2, 1).reshape(2, FT, P, 8)
    st = st.reshape(2, NB, 2, 2, FT, P)
    vec[..., 8:40] = st.transpose(0, 4, 5, 3, 1, 2).reshape(2, FT, P, 32)
    r["ffv"] = vec
    return r


_OUTS = {"o_y": (P, KT, T), "o_shift": (P, KT, 1 + NB), "o_state": (PAIRS, P, 9, HD),
         "o_k": (3 * AP_, P, T), "o_v": (3 * AP_, P, T), "o_conv": (2, 2 * FT, P, 2 + 2 * NB)}


def kernel(**inputs):
    import concourse.bacc as bacc
    from concourse.bass_utils import run_bass_kernel_spmd

    inp = {n: np.asarray(v) for n, v in inputs.items()}
    x = np.concatenate([inp["x_prompt"][0], inp["x_sample"].reshape(NB * NS, D)])
    arrays = {"xT": _channels(x), "ng": _by_channel(inp["norm_g"])}
    arrays |= _constants() | _rwkv_arrays(inp) | _attention_arrays(inp) | _ffn_arrays(inp)
    nc = bacc.Bacc("TRN2", target_bir_lowering=False, num_devices=1)
    aps = {n: nc.dram_tensor(n, list(v.shape), F32, kind="ExternalInput").ap() for n, v in arrays.items()}
    aps |= {n: nc.dram_tensor(n, list(s), F32, kind="ExternalOutput").ap() for n, s in _OUTS.items()}
    hybrid_step(nc, aps)
    o = run_bass_kernel_spmd(nc, [arrays], core_ids=[0]).results[0]

    y = o["o_y"].transpose(2, 1, 0).reshape(T, D)
    sh = o["o_shift"].transpose(2, 1, 0).reshape(1 + NB, D)
    st = o["o_state"].reshape(PAIRS, 2, HD, 9, HD).transpose(3, 0, 1, 4, 2).reshape(9, 2 * PAIRS, HD, HD)
    conv = o["o_conv"].reshape(2, 2 * DFF, 2 + 2 * NB)
    kv = [np.stack([o[n].reshape(3, 2 * AP_, HD, T)[g].transpose(2, 0, 1) for n in ("o_k", "o_v")], 1) for g in range(3)]
    c = np.ascontiguousarray
    p_kv = [c(kv[g][SEQ - min(w, SEQ):SEQ])[None, None] for g, (w, _d) in enumerate(GROUPS3)]
    s_kv = [c(kv[g][SEQ:]).reshape(1, NB, NS, 2, 2 * AP_, HD) for g in range(3)]
    return (c(y[0:SEQ])[None], c(y[SEQ:]).reshape(NB, NS, D), c(sh[0])[None, None], c(st[8])[None, None], *p_kv,
            c(conv[:, :, 0:2].transpose(0, 2, 1))[:, None], c(sh[1:])[None], c(st[0:8])[None], *s_kv,
            c(conv[:, :, 2:].reshape(2, 2 * DFF, NB, 2).transpose(0, 2, 3, 1)))
```
